# Optimizing a Trainium2 kernel written in Bass

```python
import jax, jax.numpy as jnp
from jax import lax
import numpy as np

D_MODEL = 1024
BATCH = 1
SEQ = 2048
DEPTH = 1

CONV_GROUPS = 16
CONV_GROUP_DIM = 64
D_CONV = CONV_GROUPS * CONV_GROUP_DIM
CONV_WIDTH = 3
N_Q_HEADS = 16
N_KV_HEADS = 2
HEAD_DIM = 64
Q_PER_KV = N_Q_HEADS // N_KV_HEADS
D_ATTN = N_Q_HEADS * HEAD_DIM
D_KV = N_KV_HEADS * HEAD_DIM
WINDOW = 128
BLOCK = 128
D_MIX = D_CONV + D_ATTN
D_IN_PROJ = 4 * D_CONV + 2 * D_ATTN + 2 * D_KV
SPLIT_POINTS = (D_CONV, 2 * D_CONV, 3 * D_CONV, 4 * D_CONV,
                4 * D_CONV + D_ATTN,
                4 * D_CONV + D_ATTN + D_KV,
                4 * D_CONV + D_ATTN + 2 * D_KV)
RMS_EPS = 1e-5

kernel_name = "hybrid_shortconv_swa_sink_alibi_parallel"

def rms_norm(x, gain):
    xf = x.astype(jnp.float32)
    y = xf * lax.rsqrt(jnp.mean(xf * xf, axis=-1, keepdims=True) + RMS_EPS)
    return (y * gain.astype(jnp.float32)).astype(x.dtype)

def alibi_slopes(n_heads):
    return jnp.exp2(-8.0 * jnp.arange(1, n_heads + 1, dtype=jnp.float32) / n_heads)

def short_conv(u, w):
    k = w[:, None, :].astype(u.dtype)
    return lax.conv_general_dilated(
        u, k, window_strides=(1,), padding=[(CONV_WIDTH - 1, 0)],
        dimension_numbers=("NWC", "WIO", "NWC"), feature_group_count=u.shape[-1])

def sliding_window_attention(q, k, v, sinks):
    bsz, seq, _ = q.shape
    nb = seq // BLOCK
    q = q.reshape(bsz, nb, BLOCK, N_KV_HEADS, Q_PER_KV, HEAD_DIM)
    k = k.reshape(bsz, nb, BLOCK, N_KV_HEADS, HEAD_DIM)
    v = v.reshape(bsz, nb, BLOCK, N_KV_HEADS, HEAD_DIM)
    pad = ((0, 0), (1, 0), (0, 0), (0, 0), (0, 0))
    k_band = jnp.concatenate([jnp.pad(k, pad)[:, :-1], k], axis=2)
    v_band = jnp.concatenate([jnp.pad(v, pad)[:, :-1], v], axis=2)
    scores = jnp.einsum("bnqhgd,bnkhd->bnhgqk", q, k_band).astype(jnp.float32)
    scores = scores * (HEAD_DIM ** -0.5)
    qi = jnp.arange(BLOCK)
    kj = jnp.arange(2 * BLOCK)
    dist = BLOCK + qi[:, None] - kj[None, :]
    key_pos = jnp.arange(nb)[:, None] * BLOCK - BLOCK + kj[None, :]
    valid = ((dist >= 0) & (dist < WINDOW))[None, :, :] & (key_pos >= 0)[:, None, :]
    slopes = alibi_slopes(N_Q_HEADS).reshape(N_KV_HEADS, Q_PER_KV)
    alibi = -slopes[:, :, None, None] * dist.astype(jnp.float32)
    scores = jnp.where(valid[None, :, None, None], scores + alibi[None, None], -jnp.inf)
    sink = sinks.astype(jnp.float32).reshape(N_KV_HEADS, Q_PER_KV)[None, None, :, :, None, None]
    m = jnp.maximum(jnp.max(scores, axis=-1, keepdims=True), sink)
    p = jnp.exp(scores - m)
    denom = jnp.sum(p, axis=-1, keepdims=True) + jnp.exp(sink - m)
    probs = (p / denom).astype(v.dtype)
    out = jnp.einsum("bnhgqk,bnkhd->bnqhgd", probs, v_band)
    return out.reshape(bsz, seq, D_ATTN)

def setup_inputs(seed: int = 0) -> dict:
    key = jax.random.key(seed)
    ks = jax.random.split(key, 10)
    f32 = jnp.float32
    x = jax.random.normal(ks[0], (BATCH, SEQ, D_MODEL), f32)
    norm_in = 1.0 + 0.1 * jax.random.normal(ks[1], (DEPTH, D_MODEL), f32)
    w_in = jax.random.normal(ks[2], (DEPTH, D_MODEL, D_IN_PROJ), f32) * D_MODEL ** -0.5
    conv_w = jax.random.normal(ks[3], (DEPTH, CONV_WIDTH, D_CONV), f32) * CONV_WIDTH ** -0.5
    attn_sinks = jax.random.normal(ks[4], (DEPTH, N_Q_HEADS), f32)
    norm_conv_out = 1.0 + 0.1 * jax.random.normal(ks[5], (DEPTH, D_CONV), f32)
    norm_attn_out = 1.0 + 0.1 * jax.random.normal(ks[6], (DEPTH, D_ATTN), f32)
    w_out = jax.random.normal(ks[7], (DEPTH, D_MIX, D_MODEL), f32) * D_MIX ** -0.5
    norm_final = 1.0 + 0.1 * jax.random.normal(ks[8], (D_MODEL,), f32)
    return {"x": x, "norm_in": norm_in, "w_in": w_in, "conv_w": conv_w,
            "attn_sinks": attn_sinks, "norm_conv_out": norm_conv_out,
            "norm_attn_out": norm_attn_out, "w_out": w_out, "norm_final": norm_final}

def reference(x, norm_in, w_in, conv_w, attn_sinks, norm_conv_out, norm_attn_out, w_out, norm_final):
    for layer in range(DEPTH):
        h = rms_norm(x, norm_in[layer])
        proj = jnp.einsum("bsd,de->bse", h, w_in[layer])
        cb, cc, cu, gate_c, q, k, v, gate_a = jnp.split(proj, SPLIT_POINTS, axis=-1)
        conv_y = cb * short_conv(cc * cu, conv_w[layer])
        conv_y = rms_norm(conv_y, norm_conv_out[layer]) * jax.nn.silu(gate_c)
        attn_y = sliding_window_attention(q, k, v, attn_sinks[layer])
        attn_y = rms_norm(attn_y, norm_attn_out[layer]) * jax.nn.silu(gate_a)
        mixed = jnp.concatenate([conv_y, attn_y], axis=-1)
        x = x + jnp.einsum("bse,ed->bsd", mixed, w_out[layer])
    return rms_norm(x, norm_final)


_drawn_inputs = setup_inputs


def setup_inputs(seed=0):
    import zlib

    import numpy as np

    out = dict(_drawn_inputs(seed))
    spreads = {}
    factors = {}
    for name, (base, spread) in spreads.items():
        noise = np.random.default_rng([zlib.crc32(name.encode()), seed]).standard_normal(out[name].shape)
        drawn = base * np.exp(spread * noise) if base else spread * noise
        out[name] = __import__('jax').numpy.asarray(drawn.astype(out[name].dtype))
    for name, factor in factors.items():
        out[name] = (out[name] * factor).astype(out[name].dtype)
    return out
```

```python
from contextlib import ExitStack

import concourse.bass as bass
from concourse import mybir

F32 = mybir.dt.float32
F32R = mybir.dt.float32r
I32 = mybir.dt.int32
ALU = mybir.AluOpType
ACT = mybir.ActivationFunctionType

P = 128
SEQ, D_MODEL = 2048, 1024
KT = D_MODEL // P
HEADS, KV_HEADS, HD = 16, 2, 64
TILES = D_MODEL // P
PER_KV = TILES // KV_HEADS
BLOCK = 128
HALVES = 2
HALF = SEQ // HALVES
CHUNK = 512
CHUNKS = HALF // CHUNK
HBLK = HALF // BLOCK
UNIT_BLK = 2
UNITS = HBLK // UNIT_BLK
XT = HALF // P
TT = SEQ // P
MIX_KT = 2 * TILES
EPS = 1e-5
MASKED = -1e30
QSCALE = HD ** -0.5

Q, C, U, B, GC, GA = range(6)
TILE_JOBS = 6
HALF_TILES = 2 + TILE_JOBS * TILES
AHEAD = 2
RING = 3
HALF_JOBS = HALF_TILES * CHUNKS
ITER_JOBS = TILE_JOBS * CHUNKS
LOAD_AHEAD = 3
SQUARE_STEPS = 4 * CHUNKS
VECTOR_STEPS = 17


def build(nc, x, norm_in, w_in, conv_w, sinks, gain_conv, gain_attn, w_out, norm_final, out):
    ctx = ExitStack()
    with ctx:
        def sem(name):
            return ctx.enter_context(nc.semaphore(name))

        def sems(name, n):
            return [sem(f"{name}{i}") for i in range(n)]

        mixed_dram = nc.dram_tensor("mixed", [TT, P, MIX_KT, P], F32, kind="Internal").ap()

        ident = ctx.enter_context(nc.sbuf_tensor("ident", [P, P], F32))
        ones = ctx.enter_context(nc.sbuf_tensor("ones", [P, 1], F32))
        mix_ssq = ctx.enter_context(nc.sbuf_tensor("mix_ssq", [P, 2, TT], F32))

        phase_a(nc, sem, sems, x, norm_in, w_in, conv_w, sinks, gain_conv, gain_attn,
                mixed_dram, ident, ones, mix_ssq)
        phase_b(nc, sem, sems, x, w_out, norm_final, out, mixed_dram, mix_ssq)


def phase_a(nc, sem, sems, x, norm_in, w_in, conv_w, sinks, gain_conv, gain_attn,
            mixed_dram, ident, ones, mix_ssq):
    ctx = ExitStack()
    with ctx:
        def sb(name, shape, dt=F32):
            return ctx.enter_context(nc.sbuf_tensor(name, shape, dt))

        def pb(name, shape):
            return ctx.enter_context(nc.psum_tensor(name, shape, F32))

        hT_hi = sb("hT_hi", [P, KT, HALF], F32R)
        hT_lo = sb("hT_lo", [P, KT, HALF], F32R)
        keys = sb("keys", [P, KV_HEADS, 2, (HBLK + 1) * BLOCK], F32R)
        vals = sb("vals", [P, HBLK + 1, KV_HEADS, 2, HD], F32R)
        qs = sb("qs", [P, 2, HALF], F32R)
        w_raw = sb("w_raw", [P, RING, KT, P])
        w_hi = sb("w_hi", [P, RING, KT, P], F32R)
        w_lo = sb("w_lo", [P, RING, KT, P], F32R)
        gain_in = sb("gain_in", [P, D_MODEL])
        x_sb = sb("x_sb", [P, 2, D_MODEL])
        x_stat = sb("x_stat", [P, XT, 4])
        c_sb = sb("c_sb", [P, CHUNKS, CHUNK])
        cu = sb("cu", [P, 2 + HALF])
        cu_halo = sb("cu_halo", [P, TILES, 2])
        taps = sb("taps", [P, CHUNK])
        conv_y = sb("conv_y", [P, CHUNKS, CHUNK])
        attn_y = sb("attn_y", [P, CHUNKS, CHUNK])
        tanh_sb = sb("tanh_sb", [P, CHUNKS, CHUNK])
        gated = sb("gated", [P, CHUNKS, CHUNK])
        square = sb("square", [P, CHUNK])
        ssq_conv = sb("ssq_conv", [P, CHUNKS, CHUNK])
        ssq_attn = sb("ssq_attn", [P, CHUNKS, CHUNK])
        bias = sb("bias", [P, 2, 2, 2 * BLOCK])
        probs = sb("probs", [P, 2, 2, UNIT_BLK, 2 * BLOCK])
        pT_hi = sb("pT_hi", [P, UNIT_BLK, 4 * BLOCK], F32R)
        pT_lo = sb("pT_lo", [P, UNIT_BLK, 4 * BLOCK], F32R)
        o_shift = sb("o_shift", [P, UNIT_BLK, BLOCK])
        smax = sb("smax", [P, 2, 6, 4])
        sink_bc = sb("sink_bc", [P, HEADS])
        sink_now = sb("sink_now", [P, 2, UNIT_BLK])
        conv_sb = sb("conv_sb", [P, TILES, 3])
        gains = sb("gains", [P, 2, TILES])
        vT = tanh_sb
        dist = w_raw[:, 2, 0:2, :].bitcast(I32)
        ROWMAX, MAX, NEGMAX, SINKDIFF, ROWSUM, SINKEXP = range(6)

        job_bank = [pb(f"job_bank{i}", [P, CHUNK]) for i in range(RING)]
        score_bank = [pb(f"score_bank{i}", [P, UNIT_BLK, 2 * BLOCK]) for i in range(2)]
        turn_bank = [pb(f"turn_bank{i}", [P, 4 * BLOCK]) for i in range(2)]
        out_bank = pb("out_bank", [P, UNIT_BLK, 2, BLOCK])
        x_bank = [score_bank[0][:].rearrange("p a b -> p (a b)"), score_bank[1][:].rearrange("p a b -> p (a b)"),
                  turn_bank[0][:], turn_bank[1][:]]

        consts_landed = sem("consts_landed")
        pool_set = sem("pool_set")
        bias_set = sem("bias_set")
        x_landed = sems("x_landed", 2)
        x_squared = sem("x_squared")
        x_rooted = sem("x_rooted")
        x_var = sem("x_var")
        x_scaled = sem("x_scaled")
        x_turned = sem("x_turned")
        h_hi_ready = sem("h_hi_ready")
        h_ready = sem("h_ready")
        w_landed = sems("w_landed", RING)
        w_hi_ready = sem("w_hi_ready")
        w_ready = sem("w_ready")
        job_done = sem("job_done")
        evacuated = sems("evacuated", RING)
        k_hi_ready = sem("k_hi_ready")
        k_ready = sem("k_ready")
        v_turned = sem("v_turned")
        v_hi_ready = sem("v_hi_ready")
        v_ready = sem("v_ready")
        q_hi_ready = sem("q_hi_ready")
        scores_done = sem("scores_done")
        scores_read = sem("scores_read")
        unit_begun = sem("unit_begun")
        max_ready = sem("max_ready")
        exp_done = sem("exp_done")
        rinv_ready = sem("rinv_ready")
        probs_ready = sem("probs_ready")
        probs_turned = sem("probs_turned")
        pT_hi_ready = sem("pT_hi_ready")
        pT_ready = sem("pT_ready")
        pv_done = sem("pv_done")
        shifted = sem("shifted")
        attn_ready = sem("attn_ready")
        tanh_ready = sem("tanh_ready")
        gated_ready = sem("gated_ready")
        stored = sems("stored", CHUNKS)
        squares_step = sem("squares_step")
        dve_step = sem("dve_step")
        mix_summed = sem("mix_summed")
        mix_read = sem("mix_read")

        def job_no(hf, it, j, ch):
            return hf * HALF_JOBS + 2 * CHUNKS + ITER_JOBS * it + CHUNKS * j + ch

        def job_slot(hf, j, ch):
            return (hf * HALF_JOBS + 2 * CHUNKS + CHUNKS * j + ch) % RING

        def evac_count(hf, it, j, ch):
            return (hf * HALF_JOBS + 2 * CHUNKS + CHUNKS * j + ch) // RING + 1 + ITER_JOBS // RING * it

        def tile_slot(hf, j):
            return (hf * HALF_TILES + 2 + j) % RING

        def tile_no(hf, it, j):
            return hf * HALF_TILES + 2 + TILE_JOBS * it + j

        def landed_count(hf, it, j):
            return 16 * ((hf * HALF_TILES + 2 + j) // RING + 1) + 16 * (TILE_JOBS // RING) * it

        def unit_no(hf, it, u):
            return hf * UNITS * TILES + u + UNITS * it

        def squares_count(hf, it):
            return hf + 1 + SQUARE_STEPS * (hf * TILES + it)

        def gated_count(hf, it, k):
            return 2 * CHUNKS * (hf * TILES + it) + k + 1

        block = ctx.enter_context(nc.Block())

        @block.sync
        def _(sp):
            def load_x(hf, t):
                n = hf * XT + t
                if n >= 2:
                    sp.wait_ge(x_turned, 2 * (n - 1))
                sp.dma_start(x_sb[:, n % 2, :], x[n * P:(n + 1) * P, :]).then_inc(x_landed[n % 2], 16)

            def load_w(n):
                if n >= RING:
                    sp.wait_ge(w_ready, n - RING + 1)
                sp.dma_start(w_raw[:, n % RING, :, :].rearrange("p k c -> p (k c)"), w_in[n % HALF_TILES]
                             ).then_inc(w_landed[n % RING], 16)

            load_x(0, 0)
            load_x(0, 1)
            sp.dma_start(gain_in[:], norm_in.to_broadcast([P, D_MODEL])).then_inc(consts_landed, 16)
            sp.dma_start(sink_bc[:], sinks.to_broadcast([P, HEADS])).then_inc(consts_landed, 16)
            sp.dma_start(conv_sb[:], conv_w).then_inc(consts_landed, 16)
            sp.dma_start(gains[:, 0, :], gain_conv).then_inc(consts_landed, 16)
            sp.dma_start(gains[:, 1, :], gain_attn).then_inc(consts_landed, 16)
            load_w(0)
            load_w(1)
            for hf in range(HALVES):
                for t in range(2 if hf == 0 else 0, XT):
                    load_x(hf, t)
                if hf == 0:
                    sp.wait_ge(bias_set, 1)
                    load_w(2)
                for n in range(LOAD_AHEAD, 2 + LOAD_AHEAD):
                    load_w(hf * HALF_TILES + n)
                for g in range(KV_HEADS):
                    with sp.Fori(0, PER_KV) as i4:
                        it = PER_KV * g + i4

                        def load_next(j):
                            slot = tile_slot(hf, j + LOAD_AHEAD)
                            sp.wait_ge(w_ready, tile_no(hf, it, j + LOAD_AHEAD) - RING + 1)
                            sp.dma_start(w_raw[:, slot, :, :].rearrange("p k c -> p (k c)"),
                                         w_in[2 + LOAD_AHEAD + TILE_JOBS * it + j]).then_inc(w_landed[slot], 16)

                        def store(k):
                            sp.wait_ge(gated_ready, gated_count(hf, it, k))
                            ch = k % CHUNKS
                            t0 = (hf * CHUNKS + ch) * (CHUNK // P)
                            sp.dma_start(mixed_dram[t0:t0 + CHUNK // P, :, TILES * (k // CHUNKS) + it, :].rearrange(
                                "t p c -> p t c"), gated[:, ch, :].rearrange("p (t c) -> p t c", c=P)
                                ).then_inc(stored[ch], 16)

                        for j in range(TILE_JOBS - 1):
                            load_next(j)
                        store(0)
                        load_next(TILE_JOBS - 1)
                        store(1)
                        store(2)
                        store(3)
            for k in range(CHUNKS):
                sp.wait_ge(stored[k], 16 * 2 * HALVES * TILES + 16)
            for n in range(HALVES * HALF_TILES, HALVES * HALF_TILES + RING):
                sp.wait_ge(w_landed[n % RING], 16 * (n // RING + 1))

        @block.gpsimd
        def _(pool):
            nc.gpsimd.memset(ident[:], 0.0).then_inc(pool_set, 1)
            nc.gpsimd.memset(ones[:], 1.0)
            nc.gpsimd.memset(cu_halo[:], 0.0)
            nc.gpsimd.memset(keys[:, :, :, 0:BLOCK].bitcast(F32), 0.0)
            nc.gpsimd.memset(vals[:, 0, :, :, :].bitcast(F32), 0.0)
            nc.gpsimd.iota(dist, pattern=[[-1, 2 * BLOCK]], base=BLOCK, channel_multiplier=1)
            pool.wait_ge(pool_set, 1)
            nc.gpsimd.affine_select(out=ident[:], in_=ident[:], compare_op=ALU.not_equal, fill=1.0, base=0,
                                    pattern=[[-1, P]], channel_multiplier=1).then_inc(pool_set, 1)
            pool.wait_ge(bias_set, 1)
            nc.gpsimd.affine_select(out=bias[:], in_=bias[:], compare_op=ALU.is_ge, fill=MASKED, base=BLOCK,
                                    pattern=[[0, 2], [0, 2], [-1, 2 * BLOCK]], channel_multiplier=1
                                    ).then_inc(bias_set, 1)
            pool.wait_ge(bias_set, 2)
            nc.gpsimd.affine_select(out=bias[:], in_=bias[:], compare_op=ALU.is_ge, fill=MASKED, base=-1,
                                    pattern=[[0, 2], [0, 2], [1, 2 * BLOCK]], channel_multiplier=-1
                                    ).then_inc(bias_set, 1)
            pool.wait_ge(bias_set, 3)
            nc.gpsimd.affine_select(out=bias[:, 1], in_=bias[:, 1], compare_op=ALU.is_ge, fill=MASKED,
                                    base=-BLOCK, pattern=[[0, 2], [1, 2 * BLOCK]], channel_multiplier=0
                                    ).then_inc(bias_set, 1)

            for hf in range(HALVES):
                if hf > 0:
                    pool.wait_ge(mix_summed, hf)
                nc.gpsimd.memset(ssq_conv[:], 0.0)
                nc.gpsimd.memset(ssq_attn[:], 0.0).then_inc(squares_step, 1)
                for g in range(KV_HEADS):
                    with pool.Fori(0, PER_KV) as i4:
                        it = PER_KV * g + i4

                        def normalise(u):
                            pool.wait_ge(rinv_ready, unit_no(hf, it, u) + 1)
                            nc.gpsimd.tensor_tensor(
                                probs[:, u % 2].rearrange("p h b k -> p (h b) k"),
                                probs[:, u % 2].rearrange("p h b k -> p (h b) k"),
                                smax[:, u % 2, ROWSUM, :].unsqueeze(2).to_broadcast([P, 4, 2 * BLOCK]),
                                ALU.mult).then_inc(probs_ready, 1)

                        def add_squares(src, total, ch, k):
                            pool.wait_ge(squares_step, squares_count(hf, it) + 2 * k)
                            nc.gpsimd.tensor_tensor(square[:], src[:, ch, :], src[:, ch, :],
                                                    ALU.mult).then_inc(squares_step, 1)
                            pool.wait_ge(squares_step, squares_count(hf, it) + 2 * k + 1)
                            nc.gpsimd.tensor_tensor(total[:, ch, :], total[:, ch, :], square[:],
                                                    ALU.add).then_inc(squares_step, 1)

                        normalise(0)
                        normalise(1)
                        normalise(2)
                        pool.wait_ge(evacuated[job_slot(hf, B, 0)], evac_count(hf, it, B, 0))
                        add_squares(conv_y, ssq_conv, 0, 0)
                        normalise(3)
                        pool.wait_ge(evacuated[job_slot(hf, B, 1)], evac_count(hf, it, B, 1))
                        add_squares(conv_y, ssq_conv, 1, 1)
                        pool.wait_ge(attn_ready, unit_no(hf, it, 1) + 2)
                        add_squares(attn_y, ssq_attn, 0, 2)
                        pool.wait_ge(attn_ready, unit_no(hf, it, 3) + 2)
                        add_squares(attn_y, ssq_attn, 1, 3)

        @block.scalar
        def _(act):
            def split_w(n_wait, slot, landed, used):
                act.wait_ge(w_landed[slot], landed)
                if used is not None:
                    act.wait_ge(job_done, used)
                nc.scalar.activation(w_hi[:, slot], w_raw[:, slot], ACT.Copy).then_inc(w_hi_ready, 1)

            def split_w_static(n):
                split_w(None, n % RING, 16 * (n // RING + 1), CHUNKS * (n - RING + 1) if n >= RING else None)

            split_w_static(0)
            split_w_static(1)
            for hf in range(HALVES):
                def square_x(t):
                    n = hf * XT + t
                    act.wait_ge(x_landed[n % 2], 16 * (n // 2 + 1))
                    if n >= 1:
                        act.wait_ge(x_squared, n)
                    nc.scalar.activation(attn_y[:].rearrange("p a b -> p (a b)"), x_sb[:, n % 2, :], ACT.Square,
                                         accum_out=x_stat[:, t, 0:1]).then_inc(x_squared, 1)

                def root_x(t):
                    n = hf * XT + t
                    act.wait_ge(x_var, n + 1)
                    nc.scalar.activation(x_stat[:, t, 2:3], x_stat[:, t, 1:2], ACT.Sqrt).then_inc(x_rooted, 1)

                def h_hi(t):
                    n = hf * XT + t
                    for c in range(2):
                        act.wait_ge(x_turned, 2 * n + c + 1)
                        nc.scalar.activation(hT_hi[:, 4 * c:4 * c + 4, t * P:(t + 1) * P],
                                             x_bank[2 * (t % 2) + c].rearrange("p (k c) -> p k c", c=P),
                                             ACT.Copy).then_inc(h_hi_ready, 1)

                if hf > 0:
                    act.wait_ge(mix_summed, hf)
                    act.wait_ge(gated_ready, gated_count(hf, 0, -1))
                square_x(0)
                root_x(0)
                for t in range(XT):
                    if t + 1 < XT:
                        square_x(t + 1)
                        root_x(t + 1)
                    h_hi(t)
                for ch in range(CHUNKS):
                    m = hf * HALF_JOBS + ch
                    cols = slice((1 + 4 * ch) * BLOCK, (5 + 4 * ch) * BLOCK)
                    act.wait_ge(job_done, m + 1)
                    if hf > 0 and ch == 0:
                        act.wait_ge(k_ready, CHUNKS * hf + hf)
                    for g in range(KV_HEADS):
                        rows = slice(HD * g, HD * g + HD)
                        nc.scalar.activation(keys[rows, g, 0, cols], job_bank[m % RING][rows, :], ACT.Copy)
                        other = slice(HD * (1 - g), HD * (1 - g) + HD)
                        ins = nc.scalar.activation(keys[other, g, 0, cols], job_bank[m % RING][rows, :], ACT.Copy)
                    ins.then_inc(k_hi_ready, 1)
                    if ch == 0:
                        split_w_static(hf * HALF_TILES + 2)
                for ch in range(CHUNKS):
                    m = hf * HALF_JOBS + CHUNKS + ch
                    act.wait_ge(job_done, m + 1)
                    nc.scalar.activation(vT[:, ch, :], job_bank[m % RING][:], ACT.Copy
                                         ).then_inc(evacuated[m % RING], 1)
                    if ch == 0:
                        split_w_static(hf * HALF_TILES + 3)
                for ch in range(CHUNKS):
                    act.wait_ge(v_turned, hf * CHUNKS + ch + 1)
                    nc.scalar.activation(vals[:, 1 + 4 * ch:5 + 4 * ch, :, 0, :],
                                         turn_bank[ch][:].rearrange("p (b g d) -> p b g d", g=KV_HEADS, d=HD),
                                         ACT.Copy).then_inc(v_hi_ready, 1)

                for g in range(KV_HEADS):
                    with act.Fori(0, PER_KV) as i4:
                        it = PER_KV * g + i4

                        def split_next(j):
                            slot = tile_slot(hf, j + AHEAD)
                            split_w(None, slot, landed_count(hf, it, j + AHEAD),
                                    CHUNKS * (tile_no(hf, it, j + AHEAD) - RING + 1))

                        def q_hi(ch):
                            act.wait_ge(job_done, job_no(hf, it, Q, ch) + 1)
                            bank = job_bank[job_slot(hf, Q, ch)]
                            cols = slice(ch * CHUNK, (ch + 1) * CHUNK)
                            nc.scalar.activation(qs[0:HD, 0, cols], bank[0:HD, :], ACT.Copy, scale=QSCALE)
                            nc.scalar.activation(qs[HD:P, 1, cols], bank[HD:P, :], ACT.Copy, scale=QSCALE
                                                 ).then_inc(q_hi_ready, 1)

                        def copy_c(ch):
                            act.wait_ge(job_done, job_no(hf, it, C, ch) + 1)
                            bank = job_slot(hf, C, ch)
                            nc.scalar.activation(c_sb[:, ch, :], job_bank[bank][:], ACT.Copy
                                                 ).then_inc(evacuated[bank], 1)

                        def exps(u):
                            act.wait_ge(max_ready, unit_no(hf, it, u) + 1)
                            for c in range(4):
                                nc.scalar.activation(probs[:, u % 2, c // 2, c % 2, :],
                                                     probs[:, u % 2, c // 2, c % 2, :], ACT.Exp,
                                                     bias=smax[:, u % 2, NEGMAX, c:c + 1],
                                                     accum_out=smax[:, u % 2, ROWSUM, c:c + 1])
                            nc.scalar.activation(smax[:, u % 2, SINKEXP, :], smax[:, u % 2, SINKDIFF, :],
                                                 ACT.Exp).then_inc(exp_done, 1)

                        def pT_round(u):
                            act.wait_ge(pv_done, unit_no(hf, it, u) + 1)
                            act.wait_ge(probs_turned, unit_no(hf, it, u) + 3)
                            for b in range(UNIT_BLK):
                                nc.scalar.activation(pT_hi[:, b, :], turn_bank[b][:], ACT.Copy
                                                     ).then_inc(pT_hi_ready, 1)

                        def shift(u):
                            act.wait_ge(attn_ready, unit_no(hf, it, u) + 1)
                            act.wait_ge(pv_done, unit_no(hf, it, u) + 2)
                            nc.scalar.activation(o_shift[0:HD], out_bank[HD:P, :, 0, :], ACT.Copy)
                            nc.scalar.activation(o_shift[HD:P], out_bank[0:HD, :, 1, :], ACT.Copy
                                                 ).then_inc(shifted, 1)

                        def tanh_gate(j, ch):
                            if j == GC:
                                act.wait_ge(evacuated[job_slot(hf, B, ch)], evac_count(hf, it, B, ch))
                            else:
                                act.wait_ge(gated_ready, gated_count(hf, it, ch))
                            act.wait_ge(job_done, job_no(hf, it, j, ch) + 1)
                            nc.scalar.activation(tanh_sb[:, ch, :], job_bank[job_slot(hf, j, ch)][:], ACT.Tanh,
                                                 scale=0.5).then_inc(tanh_ready, 1)

                        q_hi(0)
                        split_next(0)
                        q_hi(1)
                        exps(0)
                        copy_c(0)
                        split_next(1)
                        copy_c(1)
                        exps(1)
                        split_next(2)
                        pT_round(0)
                        exps(2)
                        split_next(3)
                        shift(0)
                        pT_round(1)
                        exps(3)
                        tanh_gate(GC, 0)
                        split_next(4)
                        shift(1)
                        pT_round(2)
                        tanh_gate(GC, 1)
                        tanh_gate(GA, 0)
                        split_next(5)
                        shift(2)
                        pT_round(3)
                        tanh_gate(GA, 1)
                        shift(3)

        @block.vector
        def _(dve):
            steps = [0]

            def link(ins):
                steps[0] += 1
                ins.then_inc(dve_step, 1)
                dve.wait_ge(dve_step, steps[0])

            def split_w(n, slot):
                dve.wait_ge(w_hi_ready, n + 1)
                nc.vector.tensor_tensor(w_lo[:, slot], w_raw[:, slot], w_hi[:, slot].bitcast(F32),
                                        ALU.subtract).then_inc(w_ready, 1)

            dve.sem_inc(scores_read, 1)
            dve.sem_inc(pT_ready, 2)
            dve.sem_inc(attn_ready, 1)
            for k in range(CHUNKS):
                dve.sem_inc(stored[k], 16)
            dve.wait_ge(pool_set, 2)
            for h in range(2):
                for first in range(2):
                    ins = nc.vector.tensor_scalar(bias[:, first, h, :], dist.rearrange("p a b -> p (a b)"),
                                                  -(2.0 ** (-8.0 * (h + 1) / HEADS)), None, ALU.mult)
            ins.then_inc(bias_set, 1)
            dve.wait_ge(consts_landed, 16 * 5)
            link(nc.vector.tensor_scalar(gains[:], gains[:], 0.5, None, ALU.mult))
            split_w(0, 0)
            split_w(1, 1)
            for hf in range(HALVES):
                def variance(t):
                    n = hf * XT + t
                    dve.wait_ge(x_squared, n + 1)
                    nc.vector.tensor_scalar(x_stat[:, t, 1:2], x_stat[:, t, 0:1], 1.0 / D_MODEL, EPS,
                                            ALU.mult, ALU.add).then_inc(x_var, 1)

                def scale_x(t):
                    n = hf * XT + t
                    var, root, r = x_stat[:, t, 1:2], x_stat[:, t, 2:3], x_stat[:, t, 3:4]
                    dve.wait_ge(x_rooted, n + 1)
                    link(nc.vector.reciprocal(r, root))
                    link(nc.vector.tensor_tensor(root, r, r, ALU.mult))
                    link(nc.vector.tensor_tensor(root, root, var, ALU.mult))
                    link(nc.vector.tensor_scalar(root, root, -0.5, 1.5, ALU.mult, ALU.add))
                    link(nc.vector.tensor_tensor(r, r, root, ALU.mult))
                    nc.vector.scalar_tensor_tensor(out=x_sb[:, n % 2, :], in0=x_sb[:, n % 2, :], scalar=r,
                                                   in1=gain_in[:], op0=ALU.mult, op1=ALU.mult
                                                   ).then_inc(x_scaled, 1)

                def h_lo(t):
                    n = hf * XT + t
                    for c in range(2):
                        dve.wait_ge(h_hi_ready, 2 * n + c + 1)
                        nc.vector.tensor_tensor(hT_lo[:, 4 * c:4 * c + 4, t * P:(t + 1) * P],
                                                x_bank[2 * (t % 2) + c].rearrange("p (k c) -> p k c", c=P),
                                                hT_hi[:, 4 * c:4 * c + 4, t * P:(t + 1) * P].bitcast(F32),
                                                ALU.subtract).then_inc(h_ready, 1)

                if hf > 0:
                    dve.wait_ge(pv_done, unit_no(hf - 1, TILES - 1, UNITS - 1) + 2)
                    nc.vector.tensor_copy(keys[:, :, :, 0:BLOCK], keys[:, :, :, HBLK * BLOCK:].bitcast(F32))
                    nc.vector.tensor_copy(vals[:, 0], vals[:, HBLK].bitcast(F32)).then_inc(k_ready, 1)
                    link(nc.vector.tensor_scalar(bias[:], bias[:], 2.0 ** TILES, None, ALU.mult))
                variance(0)
                scale_x(0)
                for t in range(XT):
                    if t + 1 < XT:
                        variance(t + 1)
                        scale_x(t + 1)
                    h_lo(t)
                for ch in range(CHUNKS):
                    m = hf * HALF_JOBS + ch
                    cols = slice((1 + 4 * ch) * BLOCK, (5 + 4 * ch) * BLOCK)
                    dve.wait_ge(k_hi_ready, hf * CHUNKS + ch + 1)
                    for g in range(KV_HEADS):
                        rows = slice(HD * g, HD * g + HD)
                        ins = nc.vector.tensor_tensor(keys[rows, g, 1, cols], job_bank[m % RING][rows, :],
                                                      keys[rows, g, 0, cols].bitcast(F32), ALU.subtract)
                    ins.then_inc(evacuated[m % RING], 1)
                    dve.wait_ge(evacuated[m % RING], m // RING + 1)
                    for g in range(KV_HEADS):
                        rows = slice(HD * g, HD * g + HD)
                        other = slice(HD * (1 - g), HD * (1 - g) + HD)
                        ins = nc.vector.tensor_copy(keys[other, g, 1, cols], keys[rows, g, 1, cols].bitcast(F32))
                    ins.then_inc(k_ready, 1)
                    if ch == 0:
                        split_w(hf * HALF_TILES + 2, (hf * HALF_TILES + 2) % RING)
                split_w(hf * HALF_TILES + 3, (hf * HALF_TILES + 3) % RING)
                for ch in range(CHUNKS):
                    dve.wait_ge(v_hi_ready, hf * CHUNKS + ch + 1)
                    nc.vector.tensor_tensor(vals[:, 1 + 4 * ch:5 + 4 * ch, :, 1, :],
                                            turn_bank[ch][:].rearrange("p (b g d) -> p b g d", g=KV_HEADS, d=HD),
                                            vals[:, 1 + 4 * ch:5 + 4 * ch, :, 0, :].bitcast(F32),
                                            ALU.subtract).then_inc(v_ready, 1)

                for g in range(KV_HEADS):
                    base = steps[0]
                    with dve.Fori(0, PER_KV) as i4:
                        it = PER_KV * g + i4
                        k = [0]

                        def step(ins):
                            k[0] += 1
                            ins.then_inc(dve_step, 1)
                            dve.wait_ge(dve_step, base + k[0] + VECTOR_STEPS * i4)

                        def split_next(j):
                            split_w(tile_no(hf, it, j + AHEAD), tile_slot(hf, j + AHEAD))

                        def q_lo(ch):
                            dve.wait_ge(q_hi_ready, CHUNKS * (hf * TILES + it) + ch + 1)
                            slot = job_slot(hf, Q, ch)
                            bank = job_bank[slot]
                            cols = slice(ch * CHUNK, (ch + 1) * CHUNK)
                            nc.vector.scalar_tensor_tensor(out=qs[HD:P, 0, cols], in0=bank[0:HD, :], scalar=QSCALE,
                                                           in1=qs[0:HD, 0, cols].bitcast(F32),
                                                           op0=ALU.mult, op1=ALU.subtract)
                            nc.vector.scalar_tensor_tensor(out=qs[0:HD, 1, cols], in0=bank[HD:P, :], scalar=QSCALE,
                                                           in1=qs[HD:P, 1, cols].bitcast(F32),
                                                           op0=ALU.mult, op1=ALU.subtract
                                                           ).then_inc(evacuated[slot], 1)

                        def maxima(u, first=0):
                            dve.wait_ge(bias_set, 4)
                            dve.wait_ge(scores_done, unit_no(hf, it, u) + 1)
                            dve.wait_ge(probs_turned, unit_no(hf, it, u) + 1)
                            dve.sem_inc(unit_begun, 1)
                            st = smax[:, u % 2]
                            for c in range(4):
                                h, b = c // 2, c % 2
                                kind = 1 if (hf == 0 and u == 0 and b == 0) else 0
                                ins = nc.vector.tensor_tensor_reduce(
                                    probs[:, u % 2, h, b, :], score_bank[h][:, b, :], bias[:, kind, h, :], 1.0,
                                    MASKED, ALU.add, ALU.max, st[:, ROWMAX, c:c + 1])
                            ins.then_inc(scores_read, 1)
                            dve.wait_ge(scores_read, unit_no(hf, it, u) + 2)
                            step(nc.vector.tensor_tensor(st[:, MAX, :], st[:, ROWMAX, :],
                                                         sink_now[:].rearrange("p h b -> p (h b)"), ALU.max))
                            nc.vector.tensor_scalar(st[:, NEGMAX, :], st[:, MAX, :], -1.0, None, ALU.mult)
                            nc.vector.tensor_tensor(st[:, SINKDIFF, :], sink_now[:].rearrange("p h b -> p (h b)"),
                                                    st[:, MAX, :], ALU.subtract).then_inc(max_ready, 1)

                        def denominators(u):
                            st = smax[:, u % 2]
                            dve.wait_ge(exp_done, unit_no(hf, it, u) + 1)
                            step(nc.vector.tensor_tensor(st[:, SINKEXP, :], st[:, SINKEXP, :], st[:, ROWSUM, :],
                                                         ALU.add))
                            nc.vector.reciprocal(st[:, ROWSUM, :], st[:, SINKEXP, :]).then_inc(rinv_ready, 1)

                        def pT_rest(u):
                            for b in range(UNIT_BLK):
                                dve.wait_ge(pT_hi_ready, 2 * unit_no(hf, it, u) + b + 1)
                                nc.vector.tensor_tensor(pT_lo[:, b, :], turn_bank[b][:], pT_hi[:, b, :].bitcast(F32),
                                                        ALU.subtract).then_inc(pT_ready, 1)

                        def attn_out(u):
                            dve.wait_ge(shifted, unit_no(hf, it, u) + 1)
                            dve.wait_ge(squares_step, squares_count(hf, it))
                            ch, o = u // 2, (u % 2) * UNIT_BLK * BLOCK
                            cols = slice(o, o + UNIT_BLK * BLOCK)
                            for h in range(2):
                                rows = slice(HD * h, HD * h + HD)
                                ins = nc.vector.tensor_tensor(
                                    attn_y[rows, ch, cols].rearrange("p (b q) -> p b q", q=BLOCK),
                                    out_bank[rows, :, h, :], o_shift[rows], ALU.add)
                            ins.then_inc(attn_ready, 1)

                        def convolve(ch):
                            dve.wait_ge(evacuated[job_slot(hf, C, ch)], evac_count(hf, it, C, ch))
                            dve.wait_ge(job_done, job_no(hf, it, U, ch) + 1)
                            slot = job_slot(hf, U, ch)
                            o = ch * CHUNK
                            nc.vector.tensor_tensor(cu[:, 2 + o:2 + o + CHUNK], job_bank[slot][:], c_sb[:, ch, :],
                                                    ALU.mult).then_inc(evacuated[slot], 1)
                            dve.wait_ge(evacuated[slot], evac_count(hf, it, U, ch))
                            step(nc.vector.tensor_scalar(taps[:], cu[:, o:o + CHUNK], conv_sb[:, it, 0:1], None,
                                                         ALU.mult))
                            for d in (1, 2):
                                step(nc.vector.scalar_tensor_tensor(out=taps[:], in0=cu[:, o + d:o + d + CHUNK],
                                                                    scalar=conv_sb[:, it, d:d + 1], in1=taps[:],
                                                                    op0=ALU.mult, op1=ALU.add))

                        def times_b(ch):
                            slot = job_slot(hf, B, ch)
                            dve.wait_ge(job_done, job_no(hf, it, B, ch) + 1)
                            dve.wait_ge(squares_step, squares_count(hf, it))
                            nc.vector.tensor_tensor(conv_y[:, ch, :], job_bank[slot][:], taps[:], ALU.mult
                                                    ).then_inc(evacuated[slot], 1)
                            dve.wait_ge(evacuated[slot], evac_count(hf, it, B, ch))

                        def gate(j, ch):
                            slot = job_slot(hf, j, ch)
                            dve.wait_ge(tanh_ready, 2 * CHUNKS * (hf * TILES + it) + CHUNKS * (j - GC) + ch + 1)
                            nc.vector.scalar_tensor_tensor(out=tanh_sb[:, ch, :], in0=tanh_sb[:, ch, :], scalar=1.0,
                                                           in1=job_bank[slot][:], op0=ALU.add, op1=ALU.mult
                                                           ).then_inc(evacuated[slot], 1)
                            dve.wait_ge(evacuated[slot], evac_count(hf, it, j, ch))

                        def apply_gate(y, branch, ch):
                            dve.wait_ge(stored[ch], 16 * (2 * (hf * TILES + it) + branch + 1))
                            nc.vector.scalar_tensor_tensor(out=gated[:, ch, :], in0=y[:, ch, :],
                                                           scalar=gains[:, branch, bass.ds(it, 1)],
                                                           in1=tanh_sb[:, ch, :], op0=ALU.mult, op1=ALU.mult
                                                           ).then_inc(gated_ready, 1)

                        nc.vector.tensor_copy(sink_now[:], sink_bc[:, bass.ds(2 * it, 2)].unsqueeze(2).to_broadcast(
                            [P, 2, UNIT_BLK]))
                        step(nc.vector.tensor_copy(cu[:, 0:2], cu_halo[:, it, :]))
                        q_lo(0)
                        split_next(0)
                        q_lo(1)
                        maxima(0)
                        denominators(0)
                        split_next(1)
                        maxima(1)
                        denominators(1)
                        convolve(0)
                        split_next(2)
                        pT_rest(0)
                        maxima(2)
                        denominators(2)
                        times_b(0)
                        convolve(1)
                        split_next(3)
                        pT_rest(1)
                        attn_out(0)
                        times_b(1)
                        maxima(3)
                        denominators(3)
                        gate(GC, 0)
                        apply_gate(conv_y, 0, 0)
                        split_next(4)
                        attn_out(1)
                        pT_rest(2)
                        gate(GC, 1)
                        apply_gate(conv_y, 0, 1)
                        gate(GA, 0)
                        dve.wait_ge(attn_ready, unit_no(hf, it, 1) + 2)
                        apply_gate(attn_y, 1, 0)
                        split_next(5)
                        attn_out(2)
                        pT_rest(3)
                        gate(GA, 1)
                        attn_out(3)
                        dve.wait_ge(attn_ready, unit_no(hf, it, 3) + 2)
                        apply_gate(attn_y, 1, 1)
                        step(nc.vector.tensor_copy(cu_halo[:, it, :], cu[:, HALF:HALF + 2]))
                        step(nc.vector.tensor_scalar(bias[:], bias[:], 0.5, None, ALU.mult))
                        assert k[0] == VECTOR_STEPS
                    steps[0] += VECTOR_STEPS * PER_KV
                dve.wait_ge(mix_summed, hf + 1)
                nc.vector.tensor_copy(mix_ssq[:, :, hf * XT:(hf + 1) * XT],
                                      out_bank[:].rearrange("p a h q -> p (a h q)")[:, 0:2 * XT].rearrange(
                                          "p (s t) -> p s t", s=2)).then_inc(mix_read, 1)

        @block.tensor
        def _(pe):
            pe.sem_inc(probs_turned, 2)
            pe.sem_inc(pv_done, 1)
            pe.wait_ge(pool_set, 2)

            def job(slot, bank, ch):
                cols = slice(ch * CHUNK, (ch + 1) * CHUNK)
                for kt in range(KT):
                    for n, (w, h) in enumerate(((w_hi, hT_hi), (w_hi, hT_lo), (w_lo, hT_hi))):
                        ins = nc.tensor.matmul(job_bank[bank][:], w[:, slot, kt, :], h[:, kt, cols],
                                               start=(kt == 0 and n == 0), stop=(kt == KT - 1 and n == 2))
                ins.then_inc(job_done, 1)

            for hf in range(HALVES):
                for t in range(XT):
                    n = hf * XT + t
                    pe.wait_ge(x_scaled, n + 1)
                    if t >= 2:
                        pe.wait_ge(h_ready, 2 * (n - 1))
                    elif t == 0:
                        pe.wait_ge(scores_read, unit_no(hf, 0, 0) + 1)
                        pe.wait_ge(pT_ready, 2 * unit_no(hf, 0, 0) + 2)
                    for c in range(2):
                        for k in range(4):
                            kt = 4 * c + k
                            ins = nc.tensor.transpose(x_bank[2 * (t % 2) + c][:, k * P:(k + 1) * P],
                                                      x_sb[:, n % 2, kt * P:(kt + 1) * P], ident[:])
                        ins.then_inc(x_turned, 1)
                for tile in range(2):
                    n = hf * HALF_TILES + tile
                    pe.wait_ge(w_ready, n + 1)
                    for ch in range(CHUNKS):
                        m = n * CHUNKS + ch
                        pe.wait_ge(h_ready, 2 * (hf * XT + (ch + 1) * CHUNK // P))
                        if m >= RING:
                            pe.wait_ge(evacuated[m % RING], m // RING)
                        job(n % RING, m % RING, ch)
                for ch in range(CHUNKS):
                    m = hf * HALF_JOBS + CHUNKS + ch
                    pe.wait_ge(evacuated[m % RING], m // RING + 1)
                    for b in range(CHUNK // BLOCK):
                        ins = nc.tensor.transpose(turn_bank[ch][:, b * P:(b + 1) * P],
                                                  vT[:, ch, b * BLOCK:(b + 1) * BLOCK], ident[:])
                    ins.then_inc(v_turned, 1)
                pe.wait_ge(k_ready, CHUNKS * (hf + 1) + hf)
                pe.wait_ge(v_ready, CHUNKS * (hf + 1))
                if hf > 0:
                    pe.wait_ge(mix_read, hf)

                for g in range(KV_HEADS):
                    with pe.Fori(0, PER_KV) as i4:
                        it = PER_KV * g + i4

                        def project(j, ch):
                            if ch == 0:
                                pe.wait_ge(w_ready, tile_no(hf, it, j) + 1)
                            slot = job_slot(hf, j, ch)
                            pe.wait_ge(evacuated[slot], evac_count(hf, it, j, ch) - 1)
                            job(tile_slot(hf, j), slot, ch)

                        def scores(u):
                            pe.wait_ge(evacuated[job_slot(hf, Q, u // 2)], evac_count(hf, it, Q, u // 2))
                            pe.wait_ge(scores_read, unit_no(hf, it, u) + 1)
                            for h in range(2):
                                for b in range(UNIT_BLK):
                                    blk = UNIT_BLK * u + b
                                    for part in range(2):
                                        ins = nc.tensor.matmul(
                                            score_bank[h][:, b, :], qs[:, h, blk * BLOCK:(blk + 1) * BLOCK],
                                            keys[:, g, part, blk * BLOCK:(blk + 2) * BLOCK],
                                            start=(part == 0), stop=(part == 1))
                            ins.then_inc(scores_done, 1)

                        def turn(u):
                            pe.wait_ge(probs_ready, unit_no(hf, it, u) + 1)
                            pe.wait_ge(pT_ready, 2 * unit_no(hf, it, u) + 2)
                            for b in range(UNIT_BLK):
                                for kb in range(2):
                                    for h in range(2):
                                        o = (2 * kb + h) * BLOCK
                                        ins = nc.tensor.transpose(
                                            turn_bank[b][:, o:o + BLOCK],
                                            probs[:, u % 2, h, b, kb * BLOCK:(kb + 1) * BLOCK], ident[:])
                            ins.then_inc(probs_turned, 1)

                        def weigh(u):
                            pe.wait_ge(pT_ready, 2 * unit_no(hf, it, u) + 4)
                            pe.wait_ge(attn_ready, unit_no(hf, it, u) + 1)
                            for b in range(UNIT_BLK):
                                n = 0
                                for kb in range(2):
                                    for pT in (pT_hi, pT_lo):
                                        ins = nc.tensor.matmul(
                                            out_bank[:, b, :, :].rearrange("p h q -> p (h q)"),
                                            vals[:, UNIT_BLK * u + b + kb, g, :, :].rearrange("p s d -> p (s d)"),
                                            pT[:, b, 2 * kb * BLOCK:2 * (kb + 1) * BLOCK],
                                            start=(n == 0), stop=(n == 3))
                                        n += 1
                            ins.then_inc(pv_done, 1)

                        project(Q, 0)
                        project(Q, 1)
                        scores(0)
                        project(C, 0)
                        project(C, 1)
                        scores(1)
                        project(U, 0)
                        turn(0)
                        project(U, 1)
                        scores(2)
                        project(B, 0)
                        weigh(0)
                        turn(1)
                        project(B, 1)
                        scores(3)
                        project(GC, 0)
                        weigh(1)
                        turn(2)
                        project(GC, 1)
                        project(GA, 0)
                        weigh(2)
                        turn(3)
                        project(GA, 1)
                        weigh(3)
                pe.wait_ge(squares_step, squares_count(hf, TILES))
                pe.wait_ge(attn_ready, unit_no(hf + 1, 0, 0) + 1)
                sums = out_bank[:].rearrange("p a h q -> p (a h q)")
                for s, ssq in enumerate((ssq_conv, ssq_attn)):
                    for t in range(XT):
                        o = t % (CHUNK // P) * P
                        ins = nc.tensor.matmul(sums[:, s * XT + t:s * XT + t + 1],
                                               ssq[:, t // (CHUNK // P), o:o + P], ones[:], start=True, stop=True)
                ins.then_inc(mix_summed, 1)


def phase_b(nc, sem, sems, x, w_out, norm_final, out, mixed_dram, mix_ssq):
    ctx = ExitStack()
    NH = D_MODEL // CHUNK
    with ctx:
        def sb(name, shape, dt=F32):
            return ctx.enter_context(nc.sbuf_tensor(name, shape, dt))

        wo_raw = sb("wo_raw", [P, 2, D_MODEL])
        wo_hi = sb("wo_hi", [P, MIX_KT, D_MODEL], F32R)
        wo_lo = sb("wo_lo", [P, MIX_KT, D_MODEL], F32R)
        mix_raw = sb("mix_raw", [P, 2, MIX_KT, P])
        mix_hi = sb("mix_hi", [P, 2, MIX_KT, P], F32R)
        mix_lo = sb("mix_lo", [P, 2, MIX_KT, P], F32R)
        z = sb("z", [P, 2, D_MODEL])
        z_sq = sb("z_sq", [P, D_MODEL])
        gain_final = sb("gain_final", [P, D_MODEL])
        z_stat = sb("z_stat", [P, 2, 4])
        mix_root = sb("mix_root", [P, 2, TT])
        mix_r = sb("mix_r", [P, 2, TT])
        bank = [[[ctx.enter_context(nc.psum_tensor(f"mix_bank{p}{s}{h}", [P, CHUNK], F32)) for h in range(NH)]
                 for s in range(2)] for p in range(2)]

        gain_landed = sem("gain_landed")
        wo_landed = sems("wo_landed", 2)
        wo_hi_ready = sem("wo_hi_ready")
        wo_ready = sem("wo_ready")
        mix_landed = sems("mix_landed", 2)
        mix_hi_ready = sem("mix_hi_ready")
        mix_ready = sem("mix_ready")
        res_landed = sems("res_landed", 2)
        mix_var = sem("mix_var")
        mix_rooted = sem("mix_rooted")
        tile_done = sem("tile_done")
        z_ready = sem("z_ready")
        z_squared = sem("z_squared")
        z_var = sem("z_var")
        z_rooted = sem("z_rooted")
        y_ready = sem("y_ready")
        y_stored = sems("y_stored", 2)
        dve_b_step = sem("dve_b_step")

        block = ctx.enter_context(nc.Block())

        def tiles(eng, body):
            body(0, 0)
            body(1, 1)
            with eng.Fori(1, TT // 2 - 1) as t2:
                body(0, 2 * t2)
                body(1, 2 * t2 + 1)
            body(0, TT - 2)
            body(1, TT - 1)

        @block.sync
        def _(sp):
            def load(p, t, wait):
                if wait:
                    sp.wait_ge(mix_ready, t - 1)
                sp.dma_start(mix_raw[:, p].rearrange("q k c -> q (k c)"),
                             mixed_dram[t].rearrange("q k c -> q (k c)")).then_inc(mix_landed[p], 16)
                if wait:
                    sp.wait_ge(y_stored[p], 8 * (t - p))
                sp.dma_start(z[:, p, :], x[bass.ts(t, P), :]).then_inc(res_landed[p], 16)

            def load_wo(kt):
                if kt >= 2:
                    sp.wait_ge(wo_ready, kt - 1)
                sp.dma_start(wo_raw[:, kt % 2, :], w_out[kt]).then_inc(wo_landed[kt % 2], 16)

            load(0, 0, False)
            for kt in range(MIX_KT):
                load_wo(kt)
                if kt == 1:
                    load(1, 1, False)
                    sp.dma_start(gain_final[:], norm_final.to_broadcast([P, D_MODEL])).then_inc(gain_landed, 16)
            with sp.Fori(1, TT // 2) as t2:
                load(0, 2 * t2, True)
                load(1, 2 * t2 + 1, True)

        @block.gpsimd
        def _(pool):
            def store(p, t):
                pool.wait_ge(y_ready, t + 1)
                pool.dma_start(out[bass.ts(t, P), :], z[:, p, :]).then_inc(y_stored[p], 16)

            with pool.Fori(0, TT // 2) as t2:
                store(0, 2 * t2)
                store(1, 2 * t2 + 1)
            for p in range(2):
                pool.wait_ge(y_stored[p], 16 * (TT // 2))

        @block.scalar
        def _(act):
            def round_mix(p, t, wait):
                act.wait_ge(mix_landed[p], 8 * (t - p) + 16)
                if wait:
                    act.wait_ge(tile_done, t - 1)
                nc.scalar.activation(mix_hi[:, p], mix_raw[:, p], ACT.Copy).then_inc(mix_hi_ready, 1)

            def body(p, t):
                if not (isinstance(t, int) and t == TT - 1):
                    round_mix(1 - p, t + 1, not (isinstance(t, int) and t == 0))
                act.wait_ge(z_ready, t + 1)
                nc.scalar.activation(z_sq[:], z[:, p, :], ACT.Square, accum_out=z_stat[:, p, 0:1]
                                     ).then_inc(z_squared, 1)
                act.wait_ge(z_var, t + 1)
                nc.scalar.activation(z_stat[:, p, 2:3], z_stat[:, p, 1:2], ACT.Sqrt).then_inc(z_rooted, 1)

            act.wait_ge(mix_var, 1)
            nc.scalar.activation(mix_root[:], mix_ssq[:], ACT.Sqrt).then_inc(mix_rooted, 1)
            round_mix(0, 0, False)
            for kt in range(MIX_KT):
                act.wait_ge(wo_landed[kt % 2], 16 * (kt // 2 + 1))
                nc.scalar.activation(wo_hi[:, kt, :], wo_raw[:, kt % 2, :], ACT.Copy).then_inc(wo_hi_ready, 1)
            tiles(act, body)

        @block.vector
        def _(dve):
            def link(ins, n):
                ins.then_inc(dve_b_step, 1)
                dve.wait_ge(dve_b_step, n)

            def newton(r, root, var, base):
                link(nc.vector.reciprocal(r, root), base + 1)
                link(nc.vector.tensor_tensor(root, r, r, ALU.mult), base + 2)
                link(nc.vector.tensor_tensor(root, root, var, ALU.mult), base + 3)
                link(nc.vector.tensor_scalar(root, root, -0.5, 1.5, ALU.mult, ALU.add), base + 4)
                link(nc.vector.tensor_tensor(r, r, root, ALU.mult), base + 5)

            NEWTON = 5
            STEPS = NEWTON + 2

            def mix_rest(p, t):
                dve.wait_ge(mix_hi_ready, t + 1)
                nc.vector.tensor_tensor(mix_lo[:, p], mix_raw[:, p], mix_hi[:, p].bitcast(F32), ALU.subtract
                                        ).then_inc(mix_ready, 1)

            def body(p, t):
                if not (isinstance(t, int) and t == TT - 1):
                    mix_rest(1 - p, t + 1)
                base = NEWTON + STEPS * t
                dve.wait_ge(tile_done, t + 1)
                dve.wait_ge(res_landed[p], 8 * (t - p) + 16)
                for s in range(2):
                    for h in range(NH):
                        cols = slice(h * CHUNK, (h + 1) * CHUNK)
                        ins = nc.vector.scalar_tensor_tensor(
                            out=z[:, p, cols], in0=bank[p][s][h][:], scalar=mix_r[:, s, bass.ds(t, 1)],
                            in1=z[:, p, cols], op0=ALU.mult, op1=ALU.add)
                    if s == 0:
                        link(ins, base + 1)
                ins.then_inc(z_ready, 1)
                dve.wait_ge(z_squared, t + 1)
                nc.vector.tensor_scalar(z_stat[:, p, 1:2], z_stat[:, p, 0:1], 1.0 / D_MODEL, EPS,
                                        ALU.mult, ALU.add).then_inc(z_var, 1)
                dve.wait_ge(z_rooted, t + 1)
                newton(z_stat[:, p, 3:4], z_stat[:, p, 2:3], z_stat[:, p, 1:2], base + 1)
                nc.vector.scalar_tensor_tensor(out=z[:, p, :], in0=z[:, p, :], scalar=z_stat[:, p, 3:4],
                                               in1=gain_final[:], op0=ALU.mult, op1=ALU.mult
                                               ).then_inc(y_ready, 1)
                link(nc.vector.tensor_copy(z_stat[:, p, 0:1], z_stat[:, p, 3:4]), base + STEPS)

            nc.vector.tensor_scalar(mix_ssq[:], mix_ssq[:], 1.0 / D_MODEL, EPS, ALU.mult, ALU.add
                                    ).then_inc(mix_var, 1)
            mix_rest(0, 0)
            dve.wait_ge(mix_rooted, 1)
            newton(mix_r[:], mix_root[:], mix_ssq[:], 0)
            for kt in range(MIX_KT):
                dve.wait_ge(wo_hi_ready, kt + 1)
                nc.vector.tensor_tensor(wo_lo[:, kt, :], wo_raw[:, kt % 2, :], wo_hi[:, kt, :].bitcast(F32),
                                        ALU.subtract).then_inc(wo_ready, 1)
            dve.wait_ge(gain_landed, 16)
            tiles(dve, body)

        @block.tensor
        def _(pe):
            def body(p, t):
                pe.wait_ge(mix_ready, t + 1)
                if not (isinstance(t, int) and t < 2):
                    pe.wait_ge(z_ready, t - 1)
                for kt in range(MIX_KT):
                    if isinstance(t, int) and t == 0:
                        pe.wait_ge(wo_ready, kt + 1)
                    s = kt // TILES
                    for n, (m, w) in enumerate(((mix_hi, wo_hi), (mix_hi, wo_lo), (mix_lo, wo_hi))):
                        for h in range(NH):
                            ins = nc.tensor.matmul(bank[p][s][h][:], m[:, p, kt, :],
                                                   w[:, kt, h * CHUNK:(h + 1) * CHUNK],
                                                   start=(kt % TILES == 0 and n == 0),
                                                   stop=(kt % TILES == TILES - 1 and n == 2))
                ins.then_inc(tile_done, 1)

            tiles(pe, body)


def kernel(x, norm_in, w_in, conv_w, attn_sinks, norm_conv_out, norm_attn_out, w_out, norm_final):
    import numpy as np
    import concourse.bacc as bacc
    from concourse.bass_utils import run_bass_kernel_spmd

    kv = 5 * TILES
    order = [kv, kv + 1]
    for i in range(TILES):
        order += [4 * TILES + i, TILES + i, 2 * TILES + i, i, 3 * TILES + i, kv + 2 + i]
    order += order[:LOAD_AHEAD]
    w_tiles = np.asarray(w_in)[0].reshape(KT, P, HALF_TILES, P).transpose(2, 1, 0, 3)[order]
    arrays = {
        "x": np.asarray(x)[0],
        "norm_in": np.asarray(norm_in),
        "w_in": w_tiles.reshape(len(order), P, KT * P),
        "conv_w": np.asarray(conv_w)[0].reshape(3, TILES, P).transpose(2, 1, 0),
        "sinks": np.asarray(attn_sinks),
        "gain_conv": np.asarray(norm_conv_out)[0].reshape(TILES, P).T,
        "gain_attn": np.asarray(norm_attn_out)[0].reshape(TILES, P).T,
        "w_out": np.asarray(w_out)[0].reshape(MIX_KT, P, D_MODEL),
        "norm_final": np.asarray(norm_final)[None],
    }
    arrays = {n: np.ascontiguousarray(a) for n, a in arrays.items()}
    nc = bacc.Bacc("TRN2", target_bir_lowering=False, num_devices=1)
    args = [nc.dram_tensor(n, list(a.shape), F32, kind="ExternalInput").ap() for n, a in arrays.items()]
    out = nc.dram_tensor("out", [SEQ, D_MODEL], F32, kind="ExternalOutput").ap()
    build(nc, *args, out)
    r = run_bass_kernel_spmd(nc, [arrays], core_ids=[0])
    return r.results[0]["out"].reshape(1, SEQ, D_MODEL)
```

```python
from contextlib import ExitStack

import concourse.bass as bass
from concourse import mybir

F32 = mybir.dt.float32
F32R = mybir.dt.float32r
I32 = mybir.dt.int32
ALU = mybir.AluOpType
ACT = mybir.ActivationFunctionType

P = 128
SEQ, D_MODEL = 2048, 1024
KT = D_MODEL // P
HEADS, KV_HEADS, HD = 16, 2, 64
TILES = D_MODEL // P
PER_KV = TILES // KV_HEADS
BLOCK = 128
HALVES = 2
HALF = SEQ // HALVES
CHUNK = 512
CHUNKS = HALF // CHUNK
HBLK = HALF // BLOCK
UNIT_BLK = 2
UNITS = HBLK // UNIT_BLK
XT = HALF // P
TT = SEQ // P
MIX_KT = 2 * TILES
EPS = 1e-5
MASKED = -1e30
QSCALE = HD ** -0.5

Q, C, U, B, GC, GA = range(6)
TILE_JOBS = 6
HALF_TILES = 2 + TILE_JOBS * TILES
AHEAD = 2
LOAD_AHEAD = 3
RING = 3
HALF_JOBS = HALF_TILES * CHUNKS
KV_JOBS = 2 * CHUNKS
ITER_JOBS = TILE_JOBS * CHUNKS
JOB_ORDER = [(Q, 0), (Q, 1), (C, 0), (C, 1), (U, 0), (U, 1),
             (B, 0), (GC, 0), (GA, 0), (B, 1), (GC, 1), (GA, 1)]
KV_ORDER = [(0, 0), (1, 0), (0, 1), (1, 1)]
SQUARE_STEPS = 4 * CHUNKS
VECTOR_STEPS = 17
NEWTON = 5
WO_RAW = 3
WO_EARLY = 8


def bank_uses():
    uses, n = {}, 0
    for hf in range(HALVES):
        for i, (tile, ch) in enumerate(KV_ORDER):
            uses["kv", hf, tile, ch] = n
            n += 1
            for t in range(4 + 2 * i, 6 + 2 * i) if hf == 1 and i < 2 else ():
                uses["x", t, 0], uses["x", t, 1] = n, n + 1
                n += 2
        uses["tiles", hf] = n
        n += ITER_JOBS * (TILES - 1)
        for k, (j, ch) in enumerate(JOB_ORDER):
            uses["last", hf, k] = n
            n += 1
            after = {(B, 1): (0,), (GC, 1): (1,), (GA, 1): (2, 3)}.get((j, ch), ())
            for t in after if hf == 0 else ():
                uses["x", t, 0], uses["x", t, 1] = n, n + 1
                n += 2
    return uses


BANK_USE = bank_uses()


def build(nc, x, norm_in, w_in, conv_w, sinks, gain_conv, gain_attn, w_out, norm_final, out):
    ctx, ctx_a, ctx_b = ExitStack(), ExitStack(), ExitStack()
    NH = D_MODEL // CHUNK
    with ctx:
        def sem(name):
            return ctx.enter_context(nc.semaphore(name))

        def sems(name, n):
            return [sem(f"{name}{i}") for i in range(n)]

        def sb(name, shape, dt=F32):
            return ctx_a.enter_context(nc.sbuf_tensor(name, shape, dt))

        def sb_b(name, shape, dt=F32):
            return ctx_b.enter_context(nc.sbuf_tensor(name, shape, dt))

        def pb(name, shape):
            return ctx.enter_context(nc.psum_tensor(name, shape, F32))

        mixed_dram = nc.dram_tensor("mixed", [TT, P, MIX_KT, P], F32, kind="Internal").ap()

        ident = ctx.enter_context(nc.sbuf_tensor("ident", [P, P], F32))
        ones = ctx.enter_context(nc.sbuf_tensor("ones", [P, 1], F32))
        mix_ssq = ctx.enter_context(nc.sbuf_tensor("mix_ssq", [P, 2, TT], F32))
        mix_root = ctx.enter_context(nc.sbuf_tensor("mix_root", [P, 2, TT], F32))
        mix_r = ctx.enter_context(nc.sbuf_tensor("mix_r", [P, 2, TT], F32))
        z_stat = ctx.enter_context(nc.sbuf_tensor("z_stat", [P, 2, 4], F32))

        x_sb = sb("x_sb", [P, 2, D_MODEL])
        gain_in = sb("gain_in", [P, D_MODEL])
        hT_hi = sb("hT_hi", [P, KT, HALF], F32R)
        hT_lo = sb("hT_lo", [P, KT, HALF], F32R)
        w_raw = sb("w_raw", [P, RING, KT, P])
        w_hi = sb("w_hi", [P, RING, KT, P], F32R)
        w_lo = sb("w_lo", [P, RING, KT, P], F32R)
        c_sb = sb("c_sb", [P, CHUNKS, CHUNK])
        cu = sb("cu", [P, 2 + HALF])
        keys = sb("keys", [P, KV_HEADS, 2, (HBLK + 1) * BLOCK], F32R)
        vals = sb("vals", [P, HBLK + 1, KV_HEADS, 2, HD], F32R)
        qs = sb("qs", [P, 2, HALF], F32R)
        x_stat = sb("x_stat", [P, XT, 4])
        cu_halo = sb("cu_halo", [P, TILES, 2])
        taps = sb("taps", [P, CHUNK])
        conv_y = sb("conv_y", [P, CHUNKS, CHUNK])
        attn_y = sb("attn_y", [P, CHUNKS, CHUNK])
        tanh_sb = sb("tanh_sb", [P, CHUNKS, CHUNK])
        gated = sb("gated", [P, CHUNKS, CHUNK])
        square = sb("square", [P, CHUNK])
        ssq_conv = sb("ssq_conv", [P, CHUNKS, CHUNK])
        ssq_attn = sb("ssq_attn", [P, CHUNKS, CHUNK])
        bias = sb("bias", [P, 2, 2, 2 * BLOCK])
        probs = sb("probs", [P, 2, 2, UNIT_BLK, 2 * BLOCK])
        pT_hi = sb("pT_hi", [P, UNIT_BLK, 4 * BLOCK], F32R)
        pT_lo = sb("pT_lo", [P, UNIT_BLK, 4 * BLOCK], F32R)
        o_shift = sb("o_shift", [P, UNIT_BLK, BLOCK])
        smax = sb("smax", [P, 2, 6, 4])
        sink_bc = sb("sink_bc", [P, HEADS])
        sink_now = sb("sink_now", [P, 2, UNIT_BLK])
        conv_sb = sb("conv_sb", [P, TILES, 3])
        gains = sb("gains", [P, 2, TILES])
        vT = tanh_sb
        dist = w_raw[:, 2, 0:2, :].bitcast(I32)
        ROWMAX, MAX, NEGMAX, SINKDIFF, ROWSUM, SINKEXP = range(6)

        job_bank = [pb(f"job_bank{i}", [P, CHUNK]) for i in range(RING)]
        score_bank = [pb(f"score_bank{i}", [P, UNIT_BLK, 2 * BLOCK]) for i in range(2)]
        turn_bank = [pb(f"turn_bank{i}", [P, 4 * BLOCK]) for i in range(2)]
        out_bank = pb("out_bank", [P, UNIT_BLK, 2, BLOCK])
        x_bank = [score_bank[0][:].rearrange("p a b -> p (a b)"), score_bank[1][:].rearrange("p a b -> p (a b)"),
                  turn_bank[0][:], turn_bank[1][:]]

        ctx_a.close()
        wo_raw = sb_b("wo_raw", [P, WO_RAW, D_MODEL])
        wo_early = sb_b("wo_early", [P, WO_EARLY, 2, D_MODEL], F32R)
        mix_hi = sb_b("mix_hi", [P, 2, MIX_KT, P], F32R)
        mix_lo = sb_b("mix_lo", [P, 2, MIX_KT, P], F32R)
        sb_b("pad", [P, D_MODEL])
        mix_raw = sb_b("mix_raw", [P, 2, MIX_KT, P])
        wo_late = sb_b("wo_late", [P, MIX_KT - WO_EARLY, 2, D_MODEL], F32R)
        z = sb_b("z", [P, 2, D_MODEL])
        gain_final = sb_b("gain_final", [P, D_MODEL])
        ctx.callback(ctx_b.close)

        def wo_part(kt, part):
            return wo_early[:, kt, part, :] if kt < WO_EARLY else wo_late[:, kt - WO_EARLY, part, :]

        flat_out = out_bank[:].rearrange("p a h q -> p (a h q)")
        all_banks = [b[:] for b in job_bank] + x_bank + [flat_out]
        mix_bank = [[all_banks[4 * p + 2 * s:4 * p + 2 * s + 2] for s in range(2)] for p in range(2)]

        gain_landed = sem("gain_landed")
        wo_landed = sems("wo_landed", WO_RAW)
        wo_hi_ready = sem("wo_hi_ready")
        wo_ready = sem("wo_ready")
        mix_landed = sems("mix_landed", 2)
        mix_hi_ready = sem("mix_hi_ready")
        mix_ready = sem("mix_ready")
        res_landed = sems("res_landed", 2)
        mix_var = sem("mix_var")
        mix_rooted = sem("mix_rooted")
        tile_done = sem("tile_done")
        z_ready = sem("z_ready")
        z_squared = sem("z_squared")
        z_var = sem("z_var")
        z_rooted = sem("z_rooted")
        y_ready = sem("y_ready")
        y_stored = sems("y_stored", 2)

        consts_landed = sem("consts_landed")
        pool_set = sem("pool_set")
        bias_set = sem("bias_set")
        x_landed = sems("x_landed", 2)
        x_squared = sem("x_squared")
        x_rooted = sem("x_rooted")
        x_var = sem("x_var")
        x_scaled = sem("x_scaled")
        x_turned = sem("x_turned")
        h_hi_ready = sem("h_hi_ready")
        h_ready = sem("h_ready")
        w_landed = sems("w_landed", RING)
        w_hi_ready = sem("w_hi_ready")
        w_ready = sem("w_ready")
        job_done = sem("job_done")
        evacuated = sems("evacuated", RING)
        k_hi_ready = sem("k_hi_ready")
        k_ready = sem("k_ready")
        v_turned = sem("v_turned")
        v_hi_ready = sem("v_hi_ready")
        v_ready = sem("v_ready")
        q_hi_ready = sem("q_hi_ready")
        scores_done = sem("scores_done")
        scores_read = sem("scores_read")
        unit_begun = sem("unit_begun")
        max_ready = sem("max_ready")
        exp_done = sem("exp_done")
        rinv_ready = sem("rinv_ready")
        probs_ready = sem("probs_ready")
        probs_turned = sem("probs_turned")
        pT_hi_ready = sem("pT_hi_ready")
        pT_ready = sem("pT_ready")
        pv_done = sem("pv_done")
        shifted = sem("shifted")
        attn_ready = sem("attn_ready")
        tanh_ready = sem("tanh_ready")
        gated_ready = sem("gated_ready")
        stored = sems("stored", CHUNKS)
        squares_step = sem("squares_step")
        dve_step = sem("dve_step")
        mix_summed = sem("mix_summed")
        mix_read = sem("mix_read")

        def job_no(hf, it, j, ch):
            return hf * HALF_JOBS + KV_JOBS + ITER_JOBS * it + JOB_ORDER.index((j, ch))

        def kv_job_no(hf, tile, ch):
            return hf * HALF_JOBS + KV_ORDER.index((tile, ch))

        def bank_use(hf, it, j, ch):
            k = JOB_ORDER.index((j, ch))
            return BANK_USE["last", hf, k] if isinstance(it, int) else BANK_USE["tiles", hf] + k

        def job_slot(hf, it, j, ch):
            return bank_use(hf, it, j, ch) % RING

        def evac_count(hf, it, j, ch):
            count = bank_use(hf, it, j, ch) // RING + 1
            return count if isinstance(it, int) else count + ITER_JOBS // RING * it

        def tile_slot(hf, j):
            return (hf * HALF_TILES + 2 + j) % RING

        def tile_no(hf, it, j):
            return hf * HALF_TILES + 2 + TILE_JOBS * it + j

        def landed_count(hf, it, j):
            return 16 * ((hf * HALF_TILES + 2 + j) // RING + 1) + 16 * (TILE_JOBS // RING) * it

        def unit_no(hf, it, u):
            return hf * UNITS * TILES + u + UNITS * it

        def squares_count(hf, it):
            return hf + 1 + SQUARE_STEPS * (hf * TILES + it)

        def gated_count(hf, it, k):
            return 2 * CHUNKS * (hf * TILES + it) + k + 1

        def tiles_of_half(eng, run):
            with eng.Fori(0, PER_KV) as i4:
                run(i4 + 0, 0, i4)
            with eng.Fori(0, PER_KV - 1) as i4:
                run(PER_KV + i4, 1, i4)
            run(TILES - 1, 1, 0)

        def tiles_of_tokens(eng, run):
            run(0, 0)
            run(1, 1)
            with eng.Fori(1, TT // 2 - 1) as t2:
                run(0, 2 * t2)
                run(1, 2 * t2 + 1)
            run(0, TT - 2)
            run(1, TT - 1)

        def x_turn_bank(hf, t, c):
            return x_bank[2 * (t % 2) + c] if hf == 0 else job_bank[BANK_USE["x", t, c] % RING][:]

        block = ctx.enter_context(nc.Block())

        @block.sync
        def _(sp):
            def load_x(n, load):
                if 2 <= load < XT + 2:
                    sp.wait_ge(x_turned, 2 * (load - 1))
                elif XT + 2 <= load < 2 * XT + 2:
                    sp.wait_ge(x_squared, load - 1)
                elif load >= 2 * XT + 2:
                    sp.wait_ge(x_turned, 2 * (load - XT - 1))
                sp.dma_start(x_sb[:, load % 2, :], x[n * P:(n + 1) * P, :]).then_inc(x_landed[load % 2], 16)

            def load_w(n):
                if n >= RING:
                    sp.wait_ge(w_ready, n - RING + 1)
                sp.dma_start(w_raw[:, n % RING, :, :].rearrange("p k c -> p (k c)"), w_in[n % HALF_TILES]
                             ).then_inc(w_landed[n % RING], 16)

            load_x(0, 0)
            load_x(1, 1)
            sp.dma_start(gain_in[:], norm_in.to_broadcast([P, D_MODEL])).then_inc(consts_landed, 16)
            sp.dma_start(sink_bc[:], sinks.to_broadcast([P, HEADS])).then_inc(consts_landed, 16)
            sp.dma_start(conv_sb[:], conv_w).then_inc(consts_landed, 16)
            sp.dma_start(gains[:, 0, :], gain_conv).then_inc(consts_landed, 16)
            sp.dma_start(gains[:, 1, :], gain_attn).then_inc(consts_landed, 16)
            load_x(2, 2)
            load_w(0)
            load_x(3, 3)
            load_w(1)
            for t in range(4, XT):
                load_x(t, t)
            sp.wait_ge(bias_set, 1)
            load_w(2)
            for hf in range(HALVES):
                for n in range(LOAD_AHEAD, 2 + LOAD_AHEAD):
                    load_w(hf * HALF_TILES + n)

                def tile(it, g, i4):
                    last = isinstance(it, int)
                    if last and hf == 0:
                        load_x(XT, XT)
                        load_x(XT + 1, XT + 1)
                    for j in range(TILE_JOBS):
                        if last and hf == 1 and j + LOAD_AHEAD >= TILE_JOBS:
                            break
                        slot = tile_slot(hf, j + LOAD_AHEAD)
                        sp.wait_ge(w_ready, tile_no(hf, it, j + LOAD_AHEAD) - RING + 1)
                        source = 2 + LOAD_AHEAD + TILE_JOBS * it + j
                        sp.dma_start(w_raw[:, slot, :, :].rearrange("p k c -> p (k c)"),
                                     w_in[source % HALF_TILES if last else source]).then_inc(w_landed[slot], 16)
                        if last and hf == 0:
                            for t in range(2 + 2 * j, 4 + 2 * j) if j < 3 else ():
                                load_x(XT + t, XT + t)
                            if j == 3:
                                load_x(XT, 2 * XT)
                                load_x(XT + 1, 2 * XT + 1)
                    if last and hf == 1:
                        for kt in range(WO_RAW):
                            load_wo(kt)
                    for k in range(2 * CHUNKS):
                        for t in {2: (2,), 3: (3, 4, 5)}.get(k, ()) if last and hf == 0 else ():
                            load_x(XT + t, 2 * XT + t)
                        sp.wait_ge(gated_ready, gated_count(hf, it, k))
                        ch, branch = k // 2, k % 2
                        t0 = (hf * CHUNKS + ch) * (CHUNK // P)
                        sp.dma_start(mixed_dram[t0:t0 + CHUNK // P, :, TILES * branch + it, :].rearrange(
                            "t p c -> p t c"), gated[:, ch, :].rearrange("p (t c) -> p t c", c=P)
                            ).then_inc(stored[ch], 16)
                        if last and hf == 1 and k == 2:
                            for ch in range(CHUNKS):
                                sp.wait_ge(stored[ch], 16 * (2 * TILES + 1))
                            load_mix(0, 0)
                    if last and hf == 0:
                        for t in range(6, XT):
                            load_x(XT + t, 2 * XT + t)

                def load_wo(kt):
                    if kt == 0:
                        sp.wait_ge(x_turned, 2 * TT)
                    if kt >= WO_RAW:
                        sp.wait_ge(wo_ready, kt - WO_RAW + 1)
                    sp.dma_start(wo_raw[:, kt % WO_RAW, :], w_out[kt]).then_inc(wo_landed[kt % WO_RAW], 16)

                def load_mix(p, t):
                    sp.dma_start(mix_raw[:, p].rearrange("q k c -> q (k c)"),
                                 mixed_dram[t].rearrange("q k c -> q (k c)")).then_inc(mix_landed[p], 16)

                def load_residual(p, t):
                    sp.dma_start(z[:, p, :], x[bass.ts(t, P), :]).then_inc(res_landed[p], 16)

                tiles_of_half(sp, tile)
            for kt in range(WO_RAW, MIX_KT):
                load_wo(kt)
                if kt == 4:
                    for ch in range(CHUNKS):
                        sp.wait_ge(stored[ch], 16 * (2 * HALVES * TILES + 1))
                    sp.wait_ge(squares_step, squares_count(HALVES - 1, TILES))
                    load_mix(1, 1)
                if kt == 8:
                    load_residual(0, 0)
                    load_residual(1, 1)
                    sp.dma_start(gain_final[:], norm_final.to_broadcast([P, D_MODEL])).then_inc(gain_landed, 16)
            with sp.Fori(1, TT // 2) as t2:
                for p in range(2):
                    sp.wait_ge(mix_ready, 2 * t2 + p - 1)
                    load_mix(p, 2 * t2 + p)
                    sp.wait_ge(y_stored[p], 16 * t2)
                    load_residual(p, 2 * t2 + p)

        @block.gpsimd
        def _(pool):
            nc.gpsimd.memset(ident[:], 0.0).then_inc(pool_set, 1)
            nc.gpsimd.memset(ones[:], 1.0)
            nc.gpsimd.memset(cu_halo[:], 0.0)
            nc.gpsimd.memset(keys[:, :, :, 0:BLOCK].bitcast(F32), 0.0)
            nc.gpsimd.memset(vals[:, 0, :, :, :].bitcast(F32), 0.0)
            nc.gpsimd.iota(dist, pattern=[[-1, 2 * BLOCK]], base=BLOCK, channel_multiplier=1)
            pool.wait_ge(pool_set, 1)
            nc.gpsimd.affine_select(out=ident[:], in_=ident[:], compare_op=ALU.not_equal, fill=1.0, base=0,
                                    pattern=[[-1, P]], channel_multiplier=1).then_inc(pool_set, 1)
            pool.wait_ge(bias_set, 1)
            nc.gpsimd.affine_select(out=bias[:], in_=bias[:], compare_op=ALU.is_ge, fill=MASKED, base=BLOCK,
                                    pattern=[[0, 2], [0, 2], [-1, 2 * BLOCK]], channel_multiplier=1
                                    ).then_inc(bias_set, 1)
            pool.wait_ge(bias_set, 2)
            nc.gpsimd.affine_select(out=bias[:], in_=bias[:], compare_op=ALU.is_ge, fill=MASKED, base=-1,
                                    pattern=[[0, 2], [0, 2], [1, 2 * BLOCK]], channel_multiplier=-1
                                    ).then_inc(bias_set, 1)
            pool.wait_ge(bias_set, 3)
            nc.gpsimd.affine_select(out=bias[:, 1], in_=bias[:, 1], compare_op=ALU.is_ge, fill=MASKED,
                                    base=-BLOCK, pattern=[[0, 2], [1, 2 * BLOCK]], channel_multiplier=0
                                    ).then_inc(bias_set, 1)

            for hf in range(HALVES):
                if hf > 0:
                    pool.wait_ge(mix_summed, hf)
                nc.gpsimd.memset(ssq_conv[:], 0.0)
                nc.gpsimd.memset(ssq_attn[:], 0.0).then_inc(squares_step, 1)

                def tile(it, g, i4):
                    def normalise(u):
                        pool.wait_ge(rinv_ready, unit_no(hf, it, u) + 1)
                        nc.gpsimd.tensor_tensor(
                            probs[:, u % 2].rearrange("p h b k -> p (h b) k"),
                            probs[:, u % 2].rearrange("p h b k -> p (h b) k"),
                            smax[:, u % 2, ROWSUM, :].unsqueeze(2).to_broadcast([P, 4, 2 * BLOCK]),
                            ALU.mult).then_inc(probs_ready, 1)

                    def add_squares(src, total, ch, k):
                        pool.wait_ge(squares_step, squares_count(hf, it) + 2 * k)
                        nc.gpsimd.tensor_tensor(square[:], src[:, ch, :], src[:, ch, :],
                                                ALU.mult).then_inc(squares_step, 1)
                        pool.wait_ge(squares_step, squares_count(hf, it) + 2 * k + 1)
                        nc.gpsimd.tensor_tensor(total[:, ch, :], total[:, ch, :], square[:],
                                                ALU.add).then_inc(squares_step, 1)

                    normalise(0)
                    normalise(1)
                    normalise(2)
                    pool.wait_ge(evacuated[job_slot(hf, it, B, 0)], evac_count(hf, it, B, 0))
                    add_squares(conv_y, ssq_conv, 0, 0)
                    normalise(3)
                    pool.wait_ge(attn_ready, unit_no(hf, it, 1) + 2)
                    add_squares(attn_y, ssq_attn, 0, 1)
                    pool.wait_ge(evacuated[job_slot(hf, it, B, 1)], evac_count(hf, it, B, 1))
                    add_squares(conv_y, ssq_conv, 1, 2)
                    pool.wait_ge(attn_ready, unit_no(hf, it, 3) + 2)
                    add_squares(attn_y, ssq_attn, 1, 3)

                tiles_of_half(pool, tile)

            with pool.Fori(0, TT // 2) as t2:
                for p in range(2):
                    pool.wait_ge(y_ready, 2 * t2 + p + 1)
                    pool.dma_start(out[bass.ts(2 * t2 + p, P), :], z[:, p, :]).then_inc(y_stored[p], 16)
            for p in range(2):
                pool.wait_ge(y_stored[p], 16 * (TT // 2))

        @block.scalar
        def _(act):
            def split_w(slot, landed, used):
                act.wait_ge(w_landed[slot], landed)
                if used is not None:
                    act.wait_ge(job_done, used)
                nc.scalar.activation(w_hi[:, slot], w_raw[:, slot], ACT.Copy).then_inc(w_hi_ready, 1)

            def square_x(t, n, load, junk):
                act.wait_ge(x_landed[load % 2], 16 * (load // 2 + 1))
                if n >= 1 and load < XT:
                    act.wait_ge(x_squared, n)
                nc.scalar.activation(junk, x_sb[:, load % 2, :], ACT.Square,
                                     accum_out=x_stat[:, t, 0:1]).then_inc(x_squared, 1)

            def h_hi(hf, t):
                n = hf * XT + t
                for c in range(2):
                    act.wait_ge(x_turned, 2 * n + c + 1)
                    nc.scalar.activation(hT_hi[:, 4 * c:4 * c + 4, t * P:(t + 1) * P],
                                         x_turn_bank(hf, t, c).rearrange("p (k c) -> p k c", c=P),
                                         ACT.Copy).then_inc(h_hi_ready, 1)

            def k_hi(hf, ch):
                slot = BANK_USE["kv", hf, 0, ch] % RING
                cols = slice((1 + 4 * ch) * BLOCK, (5 + 4 * ch) * BLOCK)
                act.wait_ge(job_done, kv_job_no(hf, 0, ch) + 1)
                if hf > 0 and ch == 0:
                    act.wait_ge(k_ready, (CHUNKS + 1) * hf)
                for g in range(KV_HEADS):
                    rows = slice(HD * g, HD * g + HD)
                    other = slice(HD * (1 - g), HD * (1 - g) + HD)
                    nc.scalar.activation(keys[rows, g, 0, cols], job_bank[slot][rows, :], ACT.Copy)
                    ins = nc.scalar.activation(keys[other, g, 0, cols], job_bank[slot][rows, :], ACT.Copy)
                ins.then_inc(k_hi_ready, 1)

            def v_copy(hf, ch):
                slot = BANK_USE["kv", hf, 1, ch] % RING
                act.wait_ge(job_done, kv_job_no(hf, 1, ch) + 1)
                nc.scalar.activation(vT[:, ch, :], job_bank[slot][:], ACT.Copy).then_inc(evacuated[slot], 1)

            def split_w_static(n, used=None):
                split_w(n % RING, 16 * (n // RING + 1), used)

            junk = attn_y[:].rearrange("p a b -> p (a b)")
            for hf in range(HALVES):
                if hf == 0:
                    def prepare(t):
                        square_x(t, t, t, junk)
                        act.wait_ge(x_var, t + 1)
                        nc.scalar.activation(x_stat[:, t, 2:3], x_stat[:, t, 1:2], ACT.Sqrt).then_inc(x_rooted, 1)
                        if t in (1, 2):
                            split_w_static(t - 1)

                    prepare(0)
                    prepare(1)
                    for t in range(4):
                        if t + 2 < XT:
                            prepare(t + 2)
                        h_hi(0, t)
                    k_hi(0, 0)
                    split_w_static(2)
                    prepare(6)
                    h_hi(0, 4)
                    prepare(7)
                    h_hi(0, 5)
                    v_copy(0, 0)
                    h_hi(0, 6)
                    h_hi(0, 7)
                else:
                    k_hi(1, 0)
                    h_hi(1, 4)
                    split_w_static(HALF_TILES + 2, HALF_JOBS)
                    h_hi(1, 5)
                    v_copy(1, 0)
                    h_hi(1, 6)
                    h_hi(1, 7)
                k_hi(hf, 1)
                split_w_static(hf * HALF_TILES + 3, kv_job_no(hf, 0, 1) + 1)
                v_copy(hf, 1)
                for ch in range(CHUNKS):
                    act.wait_ge(v_turned, hf * CHUNKS + ch + 1)
                    nc.scalar.activation(vals[:, 1 + 4 * ch:5 + 4 * ch, :, 0, :],
                                         turn_bank[ch][:].rearrange("p (b g d) -> p b g d", g=KV_HEADS, d=HD),
                                         ACT.Copy).then_inc(v_hi_ready, 1)

                def tile(it, g, i4):
                    last = isinstance(it, int)

                    def split_next(j):
                        if last and hf == HALVES - 1 and j + AHEAD >= TILE_JOBS:
                            return
                        used = {0: -1, 1: JOB_ORDER.index((Q, 1)), 2: JOB_ORDER.index((C, 1)),
                                3: JOB_ORDER.index((U, 1)), 4: JOB_ORDER.index((B, 1)),
                                5: JOB_ORDER.index((GC, 1))}[j]
                        split_w(tile_slot(hf, j + AHEAD), landed_count(hf, it, j + AHEAD),
                                job_no(hf, it, Q, 0) + used + 1)

                    def q_hi(ch):
                        act.wait_ge(job_done, job_no(hf, it, Q, ch) + 1)
                        bank = job_bank[job_slot(hf, it, Q, ch)]
                        cols = slice(ch * CHUNK, (ch + 1) * CHUNK)
                        nc.scalar.activation(qs[0:HD, 0, cols], bank[0:HD, :], ACT.Copy, scale=QSCALE)
                        nc.scalar.activation(qs[HD:P, 1, cols], bank[HD:P, :], ACT.Copy, scale=QSCALE
                                             ).then_inc(q_hi_ready, 1)

                    def copy_c(ch):
                        act.wait_ge(job_done, job_no(hf, it, C, ch) + 1)
                        slot = job_slot(hf, it, C, ch)
                        nc.scalar.activation(c_sb[:, ch, :], job_bank[slot][:], ACT.Copy).then_inc(evacuated[slot], 1)

                    def exps(u):
                        act.wait_ge(max_ready, unit_no(hf, it, u) + 1)
                        for c in range(4):
                            nc.scalar.activation(probs[:, u % 2, c // 2, c % 2, :],
                                                 probs[:, u % 2, c // 2, c % 2, :], ACT.Exp,
                                                 bias=smax[:, u % 2, NEGMAX, c:c + 1],
                                                 accum_out=smax[:, u % 2, ROWSUM, c:c + 1])
                        nc.scalar.activation(smax[:, u % 2, SINKEXP, :], smax[:, u % 2, SINKDIFF, :],
                                             ACT.Exp).then_inc(exp_done, 1)

                    def pT_round(u):
                        act.wait_ge(pv_done, unit_no(hf, it, u) + 1)
                        act.wait_ge(probs_turned, unit_no(hf, it, u) + 3)
                        for b in range(UNIT_BLK):
                            nc.scalar.activation(pT_hi[:, b, :], turn_bank[b][:], ACT.Copy).then_inc(pT_hi_ready, 1)

                    def shift(u):
                        act.wait_ge(attn_ready, unit_no(hf, it, u) + 1)
                        act.wait_ge(pv_done, unit_no(hf, it, u) + 2)
                        nc.scalar.activation(o_shift[0:HD], out_bank[HD:P, :, 0, :], ACT.Copy)
                        nc.scalar.activation(o_shift[HD:P], out_bank[0:HD, :, 1, :], ACT.Copy).then_inc(shifted, 1)

                    def tanh_gate(j, ch):
                        if j == GC:
                            act.wait_ge(evacuated[job_slot(hf, it, B, ch)], evac_count(hf, it, B, ch))
                        else:
                            act.wait_ge(gated_ready, gated_count(hf, it, 2 * ch))
                        act.wait_ge(job_done, job_no(hf, it, j, ch) + 1)
                        nc.scalar.activation(tanh_sb[:, ch, :], job_bank[job_slot(hf, it, j, ch)][:], ACT.Tanh,
                                             scale=0.5).then_inc(tanh_ready, 1)

                    ahead = last and hf == 0

                    def square_next(*tokens):
                        for t in tokens if ahead else ():
                            square_x(t, XT + t, XT + t, x_sb[:, t % 2, :])

                    q_hi(0)
                    square_next(0, 1)
                    split_next(0)
                    q_hi(1)
                    split_next(1)
                    exps(0)
                    copy_c(0)
                    square_next(2, 3)
                    copy_c(1)
                    split_next(2)
                    exps(1)
                    square_next(4, 5, 6, 7)
                    pT_round(0)
                    split_next(3)
                    exps(2)
                    if ahead:
                        act.wait_ge(x_var, XT + 1)
                        nc.scalar.activation(x_stat[:, :, 2:3], x_stat[:, :, 1:2], ACT.Sqrt).then_inc(x_rooted, 1)
                    shift(0)
                    pT_round(1)
                    tanh_gate(GC, 0)
                    exps(3)
                    tanh_gate(GA, 0)
                    shift(1)
                    pT_round(2)
                    split_next(4)
                    if ahead:
                        h_hi(1, 0)
                    tanh_gate(GC, 1)
                    split_next(5)
                    if ahead:
                        h_hi(1, 1)
                    shift(2)
                    pT_round(3)
                    tanh_gate(GA, 1)
                    if ahead:
                        h_hi(1, 2)
                        h_hi(1, 3)
                    shift(3)

                tiles_of_half(act, tile)

            def round_wo(kt):
                act.wait_ge(wo_landed[kt % WO_RAW], 16 * (kt // WO_RAW + 1))
                nc.scalar.activation(wo_part(kt, 0), wo_raw[:, kt % WO_RAW, :], ACT.Copy).then_inc(wo_hi_ready, 1)

            def round_mix(p, t, wait):
                act.wait_ge(mix_landed[p], 8 * (t - p) + 16)
                if wait:
                    act.wait_ge(tile_done, t - 1)
                nc.scalar.activation(mix_hi[:, p], mix_raw[:, p], ACT.Copy).then_inc(mix_hi_ready, 1)

            def finish(p, t):
                first, final = isinstance(t, int) and t == 0, isinstance(t, int) and t == TT - 1
                if not final:
                    round_mix(1 - p, t + 1, not first)
                if first:
                    act.wait_ge(mix_var, 1)
                    nc.scalar.activation(mix_root[:], mix_ssq[:], ACT.Sqrt).then_inc(mix_rooted, 1)
                act.wait_ge(z_ready, t + 1)
                nc.scalar.activation(wo_raw[:, 0, :], z[:, p, :], ACT.Square, accum_out=z_stat[:, p, 0:1]
                                     ).then_inc(z_squared, 1)
                act.wait_ge(z_var, t + 1)
                nc.scalar.activation(z_stat[:, p, 2:3], z_stat[:, p, 1:2], ACT.Sqrt).then_inc(z_rooted, 1)

            act.wait_ge(job_done, HALVES * HALF_JOBS)
            round_mix(0, 0, False)
            for kt in range(MIX_KT):
                if kt == WO_EARLY:
                    act.wait_ge(mix_summed, HALVES)
                    for ch in range(CHUNKS):
                        act.wait_ge(stored[ch], 16 * (2 * HALVES * TILES + 1))
                round_wo(kt)
            tiles_of_tokens(act, finish)

        @block.vector
        def _(dve):
            steps = [0]

            def link(ins):
                steps[0] += 1
                ins.then_inc(dve_step, 1)
                dve.wait_ge(dve_step, steps[0])

            def split_w(n, slot):
                dve.wait_ge(w_hi_ready, n + 1)
                nc.vector.tensor_tensor(w_lo[:, slot], w_raw[:, slot], w_hi[:, slot].bitcast(F32),
                                        ALU.subtract).then_inc(w_ready, 1)

            def newton(step, r, root, var):
                step(nc.vector.reciprocal(r, root))
                step(nc.vector.tensor_tensor(root, r, r, ALU.mult))
                step(nc.vector.tensor_tensor(root, root, var, ALU.mult))
                step(nc.vector.tensor_scalar(root, root, -0.5, 1.5, ALU.mult, ALU.add))
                step(nc.vector.tensor_tensor(r, r, root, ALU.mult))

            def variance(t, n, count):
                dve.wait_ge(x_squared, n)
                nc.vector.tensor_scalar(x_stat[:, t:t + count, 1:2], x_stat[:, t:t + count, 0:1],
                                        1.0 / D_MODEL, EPS, ALU.mult, ALU.add).then_inc(x_var, 1)

            def x_root(t, n, count):
                dve.wait_ge(x_rooted, n)
                newton(link, *(x_stat[:, t:t + count, i:i + 1] for i in (3, 2, 1)))

            def scale_x(hf, t):
                load = 2 * hf * XT + t
                dve.wait_ge(x_landed[load % 2], 16 * (load // 2 + 1))
                nc.vector.scalar_tensor_tensor(out=x_sb[:, load % 2, :], in0=x_sb[:, load % 2, :],
                                               scalar=x_stat[:, t, 3:4], in1=gain_in[:],
                                               op0=ALU.mult, op1=ALU.mult).then_inc(x_scaled, 1)

            def h_lo(hf, t):
                n = hf * XT + t
                for c in range(2):
                    dve.wait_ge(h_hi_ready, 2 * n + c + 1)
                    ins = nc.vector.tensor_tensor(hT_lo[:, 4 * c:4 * c + 4, t * P:(t + 1) * P],
                                                  x_turn_bank(hf, t, c).rearrange("p (k c) -> p k c", c=P),
                                                  hT_hi[:, 4 * c:4 * c + 4, t * P:(t + 1) * P].bitcast(F32),
                                                  ALU.subtract)
                    ins.then_inc(h_ready if hf == 0 else evacuated[BANK_USE["x", t, c] % RING], 1)

            def k_lo(hf, ch):
                use = BANK_USE["kv", hf, 0, ch]
                cols = slice((1 + 4 * ch) * BLOCK, (5 + 4 * ch) * BLOCK)
                dve.wait_ge(k_hi_ready, hf * CHUNKS + ch + 1)
                for g in range(KV_HEADS):
                    rows = slice(HD * g, HD * g + HD)
                    ins = nc.vector.tensor_tensor(keys[rows, g, 1, cols], job_bank[use % RING][rows, :],
                                                  keys[rows, g, 0, cols].bitcast(F32), ALU.subtract)
                ins.then_inc(evacuated[use % RING], 1)
                dve.wait_ge(evacuated[use % RING], use // RING + 1)
                for g in range(KV_HEADS):
                    rows = slice(HD * g, HD * g + HD)
                    other = slice(HD * (1 - g), HD * (1 - g) + HD)
                    ins = nc.vector.tensor_copy(keys[other, g, 1, cols], keys[rows, g, 1, cols].bitcast(F32))
                ins.then_inc(k_ready, 1)

            dve.sem_inc(scores_read, 1)
            dve.sem_inc(pT_ready, 2)
            dve.sem_inc(attn_ready, 1)
            for ch in range(CHUNKS):
                dve.sem_inc(stored[ch], 16)
            dve.wait_ge(consts_landed, 16 * 5)
            for hf in range(HALVES):
                if hf == 0:
                    def prepare(t):
                        variance(t, t + 1, 1)
                        x_root(t, t + 1, 1)
                        scale_x(0, t)
                        if t in (1, 2):
                            split_w(t - 1, t - 1)

                    prepare(0)
                    prepare(1)
                    for t in range(4):
                        if t + 2 < XT:
                            prepare(t + 2)
                        h_lo(0, t)
                        if t == 1:
                            dve.wait_ge(pool_set, 2)
                            for h in range(2):
                                for first in range(2):
                                    ins = nc.vector.tensor_scalar(
                                        bias[:, first, h, :], dist.rearrange("p a b -> p (a b)"),
                                        -(2.0 ** (-8.0 * (h + 1) / HEADS)), None, ALU.mult)
                            ins.then_inc(bias_set, 1)
                            link(nc.vector.tensor_scalar(gains[:], gains[:], 0.5, None, ALU.mult))
                    k_lo(0, 0)
                    split_w(2, 2)
                    prepare(6)
                    h_lo(0, 4)
                    prepare(7)
                    for t in range(5, XT):
                        h_lo(0, t)
                else:
                    dve.wait_ge(pv_done, unit_no(hf, 0, 0) + 1)
                    nc.vector.tensor_copy(keys[:, :, :, 0:BLOCK], keys[:, :, :, HBLK * BLOCK:].bitcast(F32))
                    nc.vector.tensor_copy(vals[:, 0], vals[:, HBLK].bitcast(F32)).then_inc(k_ready, 1)
                    k_lo(1, 0)
                    h_lo(1, 4)
                    scale_x(1, 6)
                    split_w(HALF_TILES + 2, (HALF_TILES + 2) % RING)
                    h_lo(1, 5)
                    scale_x(1, 7)
                    h_lo(1, 6)
                    h_lo(1, 7)
                    link(nc.vector.tensor_scalar(bias[:], bias[:], 2.0 ** TILES, None, ALU.mult))
                k_lo(hf, 1)
                split_w(hf * HALF_TILES + 3, (hf * HALF_TILES + 3) % RING)
                for ch in range(CHUNKS):
                    dve.wait_ge(v_hi_ready, hf * CHUNKS + ch + 1)
                    nc.vector.tensor_tensor(vals[:, 1 + 4 * ch:5 + 4 * ch, :, 1, :],
                                            turn_bank[ch][:].rearrange("p (b g d) -> p b g d", g=KV_HEADS, d=HD),
                                            vals[:, 1 + 4 * ch:5 + 4 * ch, :, 0, :].bitcast(F32),
                                            ALU.subtract).then_inc(v_ready, 1)
                if hf > 0:
                    dve.wait_ge(mix_summed, hf)
                    nc.vector.tensor_copy(mix_ssq[:, :, (hf - 1) * XT:hf * XT],
                                          flat_out[:, 0:2 * XT].rearrange("p (s t) -> p s t", s=2)
                                          ).then_inc(mix_read, 1)

                def tile(it, g, i4):
                    last = isinstance(it, int)
                    base = steps[0]
                    k = [0]

                    def step(ins):
                        k[0] += 1
                        ins.then_inc(dve_step, 1)
                        dve.wait_ge(dve_step, base + k[0] + VECTOR_STEPS * i4)

                    def split_next(j):
                        if not (last and hf == HALVES - 1 and j + AHEAD >= TILE_JOBS):
                            split_w(tile_no(hf, it, j + AHEAD), tile_slot(hf, j + AHEAD))

                    def q_lo(ch):
                        dve.wait_ge(q_hi_ready, CHUNKS * (hf * TILES + it) + ch + 1)
                        slot = job_slot(hf, it, Q, ch)
                        bank = job_bank[slot]
                        cols = slice(ch * CHUNK, (ch + 1) * CHUNK)
                        nc.vector.scalar_tensor_tensor(out=qs[HD:P, 0, cols], in0=bank[0:HD, :], scalar=QSCALE,
                                                       in1=qs[0:HD, 0, cols].bitcast(F32),
                                                       op0=ALU.mult, op1=ALU.subtract)
                        nc.vector.scalar_tensor_tensor(out=qs[0:HD, 1, cols], in0=bank[HD:P, :], scalar=QSCALE,
                                                       in1=qs[HD:P, 1, cols].bitcast(F32),
                                                       op0=ALU.mult, op1=ALU.subtract).then_inc(evacuated[slot], 1)

                    def maxima(u):
                        dve.wait_ge(bias_set, 4)
                        dve.wait_ge(scores_done, unit_no(hf, it, u) + 1)
                        dve.wait_ge(probs_turned, unit_no(hf, it, u) + 1)
                        dve.sem_inc(unit_begun, 1)
                        st = smax[:, u % 2]
                        for c in range(4):
                            h, b = c // 2, c % 2
                            first = 1 if (hf == 0 and u == 0 and b == 0) else 0
                            ins = nc.vector.tensor_tensor_reduce(
                                probs[:, u % 2, h, b, :], score_bank[h][:, b, :], bias[:, first, h, :], 1.0,
                                MASKED, ALU.add, ALU.max, st[:, ROWMAX, c:c + 1])
                        ins.then_inc(scores_read, 1)
                        dve.wait_ge(scores_read, unit_no(hf, it, u) + 2)
                        step(nc.vector.tensor_tensor(st[:, MAX, :], st[:, ROWMAX, :],
                                                     sink_now[:].rearrange("p h b -> p (h b)"), ALU.max))
                        nc.vector.tensor_scalar(st[:, NEGMAX, :], st[:, MAX, :], -1.0, None, ALU.mult)
                        nc.vector.tensor_tensor(st[:, SINKDIFF, :], sink_now[:].rearrange("p h b -> p (h b)"),
                                                st[:, MAX, :], ALU.subtract).then_inc(max_ready, 1)

                    def denominators(u):
                        st = smax[:, u % 2]
                        dve.wait_ge(exp_done, unit_no(hf, it, u) + 1)
                        step(nc.vector.tensor_tensor(st[:, SINKEXP, :], st[:, SINKEXP, :], st[:, ROWSUM, :],
                                                     ALU.add))
                        nc.vector.reciprocal(st[:, ROWSUM, :], st[:, SINKEXP, :]).then_inc(rinv_ready, 1)

                    def pT_rest(u):
                        for b in range(UNIT_BLK):
                            dve.wait_ge(pT_hi_ready, 2 * unit_no(hf, it, u) + b + 1)
                            nc.vector.tensor_tensor(pT_lo[:, b, :], turn_bank[b][:], pT_hi[:, b, :].bitcast(F32),
                                                    ALU.subtract).then_inc(pT_ready, 1)

                    def attn_out(u):
                        dve.wait_ge(shifted, unit_no(hf, it, u) + 1)
                        dve.wait_ge(squares_step, squares_count(hf, it))
                        ch, o = u // 2, (u % 2) * UNIT_BLK * BLOCK
                        cols = slice(o, o + UNIT_BLK * BLOCK)
                        for h in range(2):
                            rows = slice(HD * h, HD * h + HD)
                            ins = nc.vector.tensor_tensor(
                                attn_y[rows, ch, cols].rearrange("p (b q) -> p b q", q=BLOCK),
                                out_bank[rows, :, h, :], o_shift[rows], ALU.add)
                        ins.then_inc(attn_ready, 1)

                    def convolve(ch):
                        dve.wait_ge(evacuated[job_slot(hf, it, C, ch)], evac_count(hf, it, C, ch))
                        dve.wait_ge(job_done, job_no(hf, it, U, ch) + 1)
                        slot = job_slot(hf, it, U, ch)
                        o = ch * CHUNK
                        nc.vector.tensor_tensor(cu[:, 2 + o:2 + o + CHUNK], job_bank[slot][:], c_sb[:, ch, :],
                                                ALU.mult).then_inc(evacuated[slot], 1)
                        dve.wait_ge(evacuated[slot], evac_count(hf, it, U, ch))
                        step(nc.vector.tensor_scalar(taps[:], cu[:, o:o + CHUNK], conv_sb[:, it, 0:1], None,
                                                     ALU.mult))
                        for d in (1, 2):
                            step(nc.vector.scalar_tensor_tensor(out=taps[:], in0=cu[:, o + d:o + d + CHUNK],
                                                                scalar=conv_sb[:, it, d:d + 1], in1=taps[:],
                                                                op0=ALU.mult, op1=ALU.add))

                    def times_b(ch):
                        slot = job_slot(hf, it, B, ch)
                        dve.wait_ge(job_done, job_no(hf, it, B, ch) + 1)
                        dve.wait_ge(squares_step, squares_count(hf, it))
                        nc.vector.tensor_tensor(conv_y[:, ch, :], job_bank[slot][:], taps[:], ALU.mult
                                                ).then_inc(evacuated[slot], 1)
                        dve.wait_ge(evacuated[slot], evac_count(hf, it, B, ch))

                    def gate(j, ch):
                        slot = job_slot(hf, it, j, ch)
                        dve.wait_ge(tanh_ready, 2 * CHUNKS * (hf * TILES + it) + 2 * ch + (j - GC) + 1)
                        nc.vector.scalar_tensor_tensor(out=tanh_sb[:, ch, :], in0=tanh_sb[:, ch, :], scalar=1.0,
                                                       in1=job_bank[slot][:], op0=ALU.add, op1=ALU.mult
                                                       ).then_inc(evacuated[slot], 1)
                        dve.wait_ge(evacuated[slot], evac_count(hf, it, j, ch))

                    def apply_gate(y, branch, ch):
                        dve.wait_ge(stored[ch], 16 * (2 * (hf * TILES + it) + branch + 1))
                        nc.vector.scalar_tensor_tensor(out=gated[:, ch, :], in0=y[:, ch, :],
                                                       scalar=gains[:, branch, bass.ds(it, 1)],
                                                       in1=tanh_sb[:, ch, :], op0=ALU.mult, op1=ALU.mult
                                                       ).then_inc(gated_ready, 1)

                    ahead = last and hf == 0

                    nc.vector.tensor_scalar(sink_now[:], sink_bc[:, bass.ds(2 * it, 2)].unsqueeze(2).to_broadcast(
                        [P, 2, UNIT_BLK]), 1.0, None, ALU.mult)
                    step(nc.vector.tensor_scalar(cu[:, 0:2], cu_halo[:, it, :], 1.0, None, ALU.mult))
                    q_lo(0)
                    split_next(0)
                    q_lo(1)
                    split_next(1)
                    maxima(0)
                    denominators(0)
                    split_next(2)
                    maxima(1)
                    denominators(1)
                    convolve(0)
                    pT_rest(0)
                    split_next(3)
                    maxima(2)
                    if ahead:
                        variance(0, 2 * XT, XT)
                    denominators(2)
                    times_b(0)
                    convolve(1)
                    step(nc.vector.tensor_scalar(cu_halo[:, it, :], cu[:, HALF:HALF + 2], 1.0, None, ALU.mult))
                    attn_out(0)
                    pT_rest(1)
                    gate(GC, 0)
                    apply_gate(conv_y, 0, 0)
                    maxima(3)
                    denominators(3)
                    gate(GA, 0)
                    attn_out(1)
                    dve.wait_ge(attn_ready, unit_no(hf, it, 1) + 2)
                    apply_gate(attn_y, 1, 0)
                    pT_rest(2)
                    if ahead:
                        base_steps = steps[0]
                        steps[0] = base + k[0]
                        x_root(0, XT + 1, XT)
                        k[0] += NEWTON
                        steps[0] = base_steps
                        scale_x(1, 0)
                        scale_x(1, 1)
                    times_b(1)
                    split_next(4)
                    if ahead:
                        h_lo(1, 0)
                        scale_x(1, 2)
                    gate(GC, 1)
                    apply_gate(conv_y, 0, 1)
                    split_next(5)
                    if ahead:
                        h_lo(1, 1)
                        scale_x(1, 3)
                    attn_out(2)
                    pT_rest(3)
                    gate(GA, 1)
                    if ahead:
                        h_lo(1, 2)
                        scale_x(1, 4)
                        h_lo(1, 3)
                        scale_x(1, 5)
                    attn_out(3)
                    dve.wait_ge(attn_ready, unit_no(hf, it, 3) + 2)
                    apply_gate(attn_y, 1, 1)
                    step(nc.vector.tensor_scalar(bias[:], bias[:], 0.5, None, ALU.mult))
                    assert k[0] == VECTOR_STEPS + (NEWTON if ahead else 0)
                    if last:
                        steps[0] += k[0]
                    else:
                        steps[0] += VECTOR_STEPS * (PER_KV - g)

                tiles_of_half(dve, tile)

            def mix_rest(p, t):
                dve.wait_ge(mix_hi_ready, t + 1)
                nc.vector.tensor_tensor(mix_lo[:, p], mix_raw[:, p], mix_hi[:, p].bitcast(F32), ALU.subtract
                                        ).then_inc(mix_ready, 1)

            mix_rest(0, 0)
            for kt in range(MIX_KT):
                dve.wait_ge(wo_hi_ready, kt + 1)
                nc.vector.tensor_tensor(wo_part(kt, 1), wo_raw[:, kt % WO_RAW, :], wo_part(kt, 0).bitcast(F32),
                                        ALU.subtract).then_inc(wo_ready, 1)
            base_b = steps[0]

            def finish(p, t):
                first, final = isinstance(t, int) and t == 0, isinstance(t, int) and t == TT - 1
                k = [NEWTON if not first else 0]

                def step(ins):
                    k[0] += 1
                    ins.then_inc(dve_step, 1)
                    dve.wait_ge(dve_step, base_b + k[0] + (NEWTON + 2) * t)

                if not final:
                    mix_rest(1 - p, t + 1)
                if first:
                    dve.wait_ge(mix_summed, HALVES)
                    nc.vector.tensor_copy(mix_ssq[:, :, XT:TT],
                                          flat_out[:, 0:2 * XT].rearrange("p (s t) -> p s t", s=2)
                                          ).then_inc(mix_read, 1)
                    dve.wait_ge(mix_read, HALVES)
                    nc.vector.tensor_scalar(mix_ssq[:], mix_ssq[:], 1.0 / D_MODEL, EPS, ALU.mult, ALU.add
                                            ).then_inc(mix_var, 1)
                    dve.wait_ge(mix_rooted, 1)
                    newton(step, mix_r[:], mix_root[:], mix_ssq[:])
                dve.wait_ge(tile_done, t + 1)
                dve.wait_ge(res_landed[p], 8 * (t - p) + 16)
                for s in range(2):
                    for h in range(NH):
                        cols = slice(h * CHUNK, (h + 1) * CHUNK)
                        ins = nc.vector.scalar_tensor_tensor(
                            out=z[:, p, cols], in0=mix_bank[p][s][h], scalar=mix_r[:, s, bass.ds(t, 1)],
                            in1=z[:, p, cols], op0=ALU.mult, op1=ALU.add)
                    if s == 0:
                        step(ins)
                ins.then_inc(z_ready, 1)
                dve.wait_ge(z_squared, t + 1)
                nc.vector.tensor_scalar(z_stat[:, p, 1:2], z_stat[:, p, 0:1], 1.0 / D_MODEL, EPS,
                                        ALU.mult, ALU.add).then_inc(z_var, 1)
                dve.wait_ge(z_rooted, t + 1)
                newton(step, z_stat[:, p, 3:4], z_stat[:, p, 2:3], z_stat[:, p, 1:2])
                if first:
                    dve.wait_ge(gain_landed, 16)
                nc.vector.scalar_tensor_tensor(out=z[:, p, :], in0=z[:, p, :], scalar=z_stat[:, p, 3:4],
                                               in1=gain_final[:], op0=ALU.mult, op1=ALU.mult
                                               ).then_inc(y_ready, 1)
                step(nc.vector.tensor_copy(z_stat[:, p, 0:1], z_stat[:, p, 3:4]))
                assert k[0] == 2 * NEWTON + 2

            tiles_of_tokens(dve, finish)

        @block.tensor
        def _(pe):
            pe.sem_inc(probs_turned, 2)
            pe.sem_inc(pv_done, 1)
            pe.wait_ge(pool_set, 2)

            def job(slot, bank, ch):
                cols = slice(ch * CHUNK, (ch + 1) * CHUNK)
                for kt in range(KT):
                    for n, (w, h) in enumerate(((w_hi, hT_hi), (w_hi, hT_lo), (w_lo, hT_hi))):
                        ins = nc.tensor.matmul(job_bank[bank][:], w[:, slot, kt, :], h[:, kt, cols],
                                               start=(kt == 0 and n == 0), stop=(kt == KT - 1 and n == 2))
                ins.then_inc(job_done, 1)

            def turn_x(hf, t):
                n, load = hf * XT + t, 2 * hf * XT + t
                pe.wait_ge(x_scaled, n + 1)
                for c in range(2):
                    if hf == 0 and t >= 2:
                        pe.wait_ge(h_ready, 2 * (t - 1))
                    elif hf > 0:
                        use = BANK_USE["x", t, c]
                        pe.wait_ge(evacuated[use % RING], use // RING)
                    for k in range(4):
                        kt = 4 * c + k
                        ins = nc.tensor.transpose(x_turn_bank(hf, t, c)[:, k * P:(k + 1) * P],
                                                  x_sb[:, load % 2, kt * P:(kt + 1) * P], ident[:])
                    ins.then_inc(x_turned, 1)

            def kv_job(hf, tile, ch):
                n, use = hf * HALF_TILES + tile, BANK_USE["kv", hf, tile, ch]
                pe.wait_ge(w_ready, n + 1)
                if hf == 0:
                    pe.wait_ge(h_ready, 2 * (ch + 1) * CHUNK // P)
                else:
                    ready = BANK_USE["x", (ch + 1) * CHUNK // P - 1, 1]
                    pe.wait_ge(evacuated[ready % RING], ready // RING + 1)
                if use >= RING:
                    pe.wait_ge(evacuated[use % RING], use // RING)
                job(n % RING, use % RING, ch)

            def sum_squares(half):
                pe.wait_ge(squares_step, squares_count(half, TILES))
                pe.wait_ge(attn_ready, unit_no(half + 1, 0, 0) + 1)
                for s, ssq in enumerate((ssq_conv, ssq_attn)):
                    for t in range(XT):
                        o = t % (CHUNK // P) * P
                        ins = nc.tensor.matmul(flat_out[:, s * XT + t:s * XT + t + 1],
                                               ssq[:, t // (CHUNK // P), o:o + P], ones[:], start=True, stop=True)
                ins.then_inc(mix_summed, 1)

            for hf in range(HALVES):
                if hf == 0:
                    for t in range(4):
                        turn_x(0, t)
                for i, (kv, ch) in enumerate(KV_ORDER):
                    kv_job(hf, kv, ch)
                    for t in range(4 + 2 * i, 6 + 2 * i) if i < 2 else ():
                        turn_x(hf, t)
                if hf > 0:
                    sum_squares(hf - 1)
                for ch in range(CHUNKS):
                    use = BANK_USE["kv", hf, 1, ch]
                    pe.wait_ge(evacuated[use % RING], use // RING + 1)
                    pe.wait_ge(pT_ready, 2 * unit_no(hf, 0, 0) + 2)
                    for b in range(CHUNK // BLOCK):
                        ins = nc.tensor.transpose(turn_bank[ch][:, b * P:(b + 1) * P],
                                                  vT[:, ch, b * BLOCK:(b + 1) * BLOCK], ident[:])
                    ins.then_inc(v_turned, 1)

                def tile(it, g, i4):
                    last = isinstance(it, int)

                    def project(j, ch):
                        if ch == 0:
                            pe.wait_ge(w_ready, tile_no(hf, it, j) + 1)
                        slot = job_slot(hf, it, j, ch)
                        pe.wait_ge(evacuated[slot], evac_count(hf, it, j, ch) - 1)
                        job(tile_slot(hf, j), slot, ch)

                    def scores(u):
                        pe.wait_ge(k_ready, CHUNKS * (hf + 1) + hf)
                        pe.wait_ge(v_ready, CHUNKS * (hf + 1))
                        pe.wait_ge(evacuated[job_slot(hf, it, Q, u // 2)], evac_count(hf, it, Q, u // 2))
                        pe.wait_ge(scores_read, unit_no(hf, it, u) + 1)
                        for h in range(2):
                            for b in range(UNIT_BLK):
                                blk = UNIT_BLK * u + b
                                for part in range(2):
                                    ins = nc.tensor.matmul(
                                        score_bank[h][:, b, :], qs[:, h, blk * BLOCK:(blk + 1) * BLOCK],
                                        keys[:, g, part, blk * BLOCK:(blk + 2) * BLOCK],
                                        start=(part == 0), stop=(part == 1))
                        ins.then_inc(scores_done, 1)

                    def turn(u):
                        pe.wait_ge(probs_ready, unit_no(hf, it, u) + 1)
                        pe.wait_ge(pT_ready, 2 * unit_no(hf, it, u) + 2)
                        for b in range(UNIT_BLK):
                            for kb in range(2):
                                for h in range(2):
                                    o = (2 * kb + h) * BLOCK
                                    ins = nc.tensor.transpose(
                                        turn_bank[b][:, o:o + BLOCK],
                                        probs[:, u % 2, h, b, kb * BLOCK:(kb + 1) * BLOCK], ident[:])
                        ins.then_inc(probs_turned, 1)

                    def weigh(u):
                        pe.wait_ge(pT_ready, 2 * unit_no(hf, it, u) + 4)
                        pe.wait_ge(attn_ready, unit_no(hf, it, u) + 1)
                        if u == 0 and hf > 0:
                            pe.wait_ge(mix_read, hf)
                        for b in range(UNIT_BLK):
                            n = 0
                            for kb in range(2):
                                for pT in (pT_hi, pT_lo):
                                    ins = nc.tensor.matmul(
                                        out_bank[:, b, :, :].rearrange("p h q -> p (h q)"),
                                        vals[:, UNIT_BLK * u + b + kb, g, :, :].rearrange("p s d -> p (s d)"),
                                        pT[:, b, 2 * kb * BLOCK:2 * (kb + 1) * BLOCK],
                                        start=(n == 0), stop=(n == 3))
                                    n += 1
                        ins.then_inc(pv_done, 1)

                    ahead = last and hf == 0

                    project(Q, 0)
                    project(Q, 1)
                    scores(0)
                    project(C, 0)
                    project(C, 1)
                    scores(1)
                    project(U, 0)
                    turn(0)
                    project(U, 1)
                    scores(2)
                    project(B, 0)
                    weigh(0)
                    turn(1)
                    project(GC, 0)
                    scores(3)
                    project(GA, 0)
                    weigh(1)
                    turn(2)
                    project(B, 1)
                    if ahead:
                        turn_x(1, 0)
                    project(GC, 1)
                    if ahead:
                        turn_x(1, 1)
                    weigh(2)
                    turn(3)
                    project(GA, 1)
                    if ahead:
                        turn_x(1, 2)
                        turn_x(1, 3)
                    weigh(3)

                tiles_of_half(pe, tile)

            def multiply(p, t):
                first = isinstance(t, int) and t < 2
                pe.wait_ge(mix_ready, t + 1)
                if not first:
                    pe.wait_ge(z_ready, t - 1)
                elif t == 0:
                    for slot in range(RING):
                        uses = BANK_USE["last", HALVES - 1, ITER_JOBS - 1] + 1
                        pe.wait_ge(evacuated[slot], (uses - 1 - slot) // RING + 1)
                    pe.wait_ge(scores_read, unit_no(HALVES, 0, 0) + 1)
                else:
                    pe.wait_ge(pT_ready, 2 * unit_no(HALVES, 0, 0) + 2)
                    pe.wait_ge(mix_read, HALVES)
                for kt in range(MIX_KT):
                    if first and t == 0:
                        pe.wait_ge(wo_ready, kt + 1)
                    s = kt // TILES
                    for n, (m, part) in enumerate(((mix_hi, 0), (mix_hi, 1), (mix_lo, 0))):
                        for h in range(NH):
                            ins = nc.tensor.matmul(mix_bank[p][s][h], m[:, p, kt, :],
                                                   wo_part(kt, part)[:, h * CHUNK:(h + 1) * CHUNK],
                                                   start=(kt % TILES == 0 and n == 0),
                                                   stop=(kt % TILES == TILES - 1 and n == 2))
                    if first and t == 0 and kt == 2:
                        sum_squares(HALVES - 1)
                ins.then_inc(tile_done, 1)

            tiles_of_tokens(pe, multiply)


def kernel(x, norm_in, w_in, conv_w, attn_sinks, norm_conv_out, norm_attn_out, w_out, norm_final):
    import numpy as np
    import concourse.bacc as bacc
    from concourse.bass_utils import run_bass_kernel_spmd

    kv = 5 * TILES
    order = [kv, kv + 1]
    for i in range(TILES):
        order += [4 * TILES + i, TILES + i, 2 * TILES + i, i, 3 * TILES + i, kv + 2 + i]
    w_tiles = np.asarray(w_in)[0].reshape(KT, P, HALF_TILES, P).transpose(2, 1, 0, 3)[order]
    arrays = {
        "x": np.asarray(x)[0],
        "norm_in": np.asarray(norm_in),
        "w_in": w_tiles.reshape(len(order), P, KT * P),
        "conv_w": np.asarray(conv_w)[0].reshape(3, TILES, P).transpose(2, 1, 0),
        "sinks": np.asarray(attn_sinks),
        "gain_conv": np.asarray(norm_conv_out)[0].reshape(TILES, P).T,
        "gain_attn": np.asarray(norm_attn_out)[0].reshape(TILES, P).T,
        "w_out": np.asarray(w_out)[0].reshape(MIX_KT, P, D_MODEL),
        "norm_final": np.asarray(norm_final)[None],
    }
    arrays = {n: np.ascontiguousarray(a) for n, a in arrays.items()}
    nc = bacc.Bacc("TRN2", target_bir_lowering=False, num_devices=1)
    args = [nc.dram_tensor(n, list(a.shape), F32, kind="ExternalInput").ap() for n, a in arrays.items()]
    out = nc.dram_tensor("out", [SEQ, D_MODEL], F32, kind="ExternalOutput").ap()
    build(nc, *args, out)
    r = run_bass_kernel_spmd(nc, [arrays], core_ids=[0])
    return r.results[0]["out"].reshape(1, SEQ, D_MODEL)
```

```python
from contextlib import ExitStack

import concourse.bass as bass
from concourse import mybir

F32 = mybir.dt.float32
F32R = mybir.dt.float32r
I32 = mybir.dt.int32
ALU = mybir.AluOpType
ACT = mybir.ActivationFunctionType

P = 128
SEQ, D_MODEL = 2048, 1024
KT = D_MODEL // P
HEADS, KV_HEADS, HD = 16, 2, 64
TILES = D_MODEL // P
PER_KV = TILES // KV_HEADS
BLOCK = 128
HALVES = 2
HALF = SEQ // HALVES
CHUNK = 512
CHUNKS = HALF // CHUNK
HBLK = HALF // BLOCK
UNIT_BLK = 2
UNITS = HBLK // UNIT_BLK
XT = HALF // P
TT = SEQ // P
MIX_KT = 2 * TILES
EPS = 1e-5
MASKED = -1e30
QSCALE = HD ** -0.5

Q, C, U, B, GC, GA = range(6)
TILE_JOBS = 6
HALF_TILES = 2 + TILE_JOBS * TILES
AHEAD = 2
LOAD_AHEAD = 3
RING = 3
HALF_JOBS = HALF_TILES * CHUNKS
KV_JOBS = 2 * CHUNKS
ITER_JOBS = TILE_JOBS * CHUNKS
JOB_ORDER = [(Q, 0), (Q, 1), (C, 0), (C, 1), (U, 0), (U, 1),
             (B, 0), (GC, 0), (GA, 0), (B, 1), (GC, 1), (GA, 1)]
KV_ORDER = [(0, 0), (1, 0), (0, 1), (1, 1)]
X_AFTER = [(GA, 0), (B, 1), (GC, 1)]
SQUARE_STEPS = 4 * CHUNKS
VECTOR_STEPS = 17
NEWTON = 5
WO_RAW = 3
WO_EARLY = 8
GROUP_KT = 4


def bank_uses():
    uses, n = {}, 0
    for hf in range(HALVES):
        for i, (tile, ch) in enumerate(KV_ORDER):
            uses["kv", hf, tile, ch] = n
            n += 1
        uses["tiles", hf] = n
        n += ITER_JOBS * (TILES - 1)
        for k, (j, ch) in enumerate(JOB_ORDER):
            uses["last", hf, k] = n
            n += 1
            if hf == 0 and (j, ch) in X_AFTER:
                t = X_AFTER.index((j, ch))
                uses["x", t, 0], uses["x", t, 1] = n, n + 1
                n += 2
    return uses


BANK_USE = bank_uses()
X_IN_KV = [[(4, 5), (6, 7), (), ()], [(5, 6), (7,), (), ()]]
STAT_GROUPS = [(0, 1), (1, 1), (2, 2), (4, 4)]


def build(nc, x, norm_in, w_in, conv_w, sinks, gain_conv, gain_attn, w_out, norm_final, out):
    ctx, ctx_a, ctx_b = ExitStack(), ExitStack(), ExitStack()
    NH = D_MODEL // CHUNK
    with ctx:
        def sem(name):
            return ctx.enter_context(nc.semaphore(name))

        def sems(name, n):
            return [sem(f"{name}{i}") for i in range(n)]

        def sb(name, shape, dt=F32):
            return ctx_a.enter_context(nc.sbuf_tensor(name, shape, dt))

        def sb_b(name, shape, dt=F32):
            return ctx_b.enter_context(nc.sbuf_tensor(name, shape, dt))

        def pb(name, shape):
            return ctx.enter_context(nc.psum_tensor(name, shape, F32))

        mixed_dram = nc.dram_tensor("mixed", [TT, P, MIX_KT, P], F32, kind="Internal").ap()

        ident = ctx.enter_context(nc.sbuf_tensor("ident", [P, P], F32))
        in_block = ctx.enter_context(nc.sbuf_tensor("in_block", [P, 2, BLOCK], F32))
        ones = ctx.enter_context(nc.sbuf_tensor("ones", [P, 1], F32))
        mix_ssq = ctx.enter_context(nc.sbuf_tensor("mix_ssq", [P, 2, TT], F32))
        mix_root = ctx.enter_context(nc.sbuf_tensor("mix_root", [P, 2, TT], F32))
        mix_r = ctx.enter_context(nc.sbuf_tensor("mix_r", [P, 2, TT], F32))
        z_stat = ctx.enter_context(nc.sbuf_tensor("z_stat", [P, 2, 4], F32))

        x_sb = sb("x_sb", [P, 2, D_MODEL])
        gain_in = sb("gain_in", [P, D_MODEL])
        hT_hi = sb("hT_hi", [P, KT, HALF], F32R)
        hT_lo = sb("hT_lo", [P, KT, HALF], F32R)
        w_raw = sb("w_raw", [P, RING, KT, P])
        w_hi = sb("w_hi", [P, RING, KT, P], F32R)
        w_lo = sb("w_lo", [P, RING, KT, P], F32R)
        c_sb = sb("c_sb", [P, CHUNKS, CHUNK])
        cu = sb("cu", [P, 2 + HALF])
        keys = sb("keys", [P, KV_HEADS, 2, (HBLK + 1) * BLOCK], F32R)
        vals = sb("vals", [P, HBLK + 1, KV_HEADS, 2, HD], F32R)
        qs = sb("qs", [P, 2, HALF], F32R)
        x_stat = sb("x_stat", [P, XT, 4])
        cu_halo = sb("cu_halo", [P, TILES, 2])
        taps = sb("taps", [P, CHUNK])
        conv_y = sb("conv_y", [P, CHUNKS, CHUNK])
        attn_y = sb("attn_y", [P, CHUNKS, CHUNK])
        tanh_sb = sb("tanh_sb", [P, CHUNKS, CHUNK])
        gated = sb("gated", [P, CHUNKS, CHUNK])
        square = sb("square", [P, CHUNK])
        ssq_conv = sb("ssq_conv", [P, CHUNKS, CHUNK])
        ssq_attn = sb("ssq_attn", [P, CHUNKS, CHUNK])
        bias = sb("bias", [P, 2, 2, 2 * BLOCK])
        probs = sb("probs", [P, 2, 2, UNIT_BLK, 2 * BLOCK])
        pT_hi = sb("pT_hi", [P, UNIT_BLK, 4 * BLOCK], F32R)
        pT_lo = sb("pT_lo", [P, UNIT_BLK, 4 * BLOCK], F32R)
        o_shift = sb("o_shift", [P, UNIT_BLK, BLOCK])
        smax = sb("smax", [P, 2, 6, 4])
        sink_bc = sb("sink_bc", [P, HEADS])
        sink_now = sb("sink_now", [P, 2, UNIT_BLK])
        conv_sb = sb("conv_sb", [P, TILES, 3])
        gains = sb("gains", [P, 2, TILES])
        parted = probs[:].rearrange("p u h b k -> p u (h b k)").rearrange(
            "p u (b k h q) -> p u b k h q", b=UNIT_BLK, k=2, h=2)
        x_first = [x_sb[:, 0, :], x_sb[:, 1, :]] + [b[:].rearrange("p a b -> p (a b)") for b in (conv_y, gated, c_sb)] + [
            probs[:, i].rearrange("p h b k -> p (h b k)") for i in range(2)] + [
            cu[:, 0:D_MODEL]]
        vT = tanh_sb
        dist = w_raw[:, 2, 0:2, :].bitcast(I32)
        ROWMAX, MAX, NEGMAX, SINKDIFF, ROWSUM, SINKEXP = range(6)

        job_bank = [pb(f"job_bank{i}", [P, CHUNK]) for i in range(RING)]
        score_bank = [pb(f"score_bank{i}", [P, UNIT_BLK, 2 * BLOCK]) for i in range(2)]
        turn_bank = [pb(f"turn_bank{i}", [P, 4 * BLOCK]) for i in range(2)]
        out_bank = pb("out_bank", [P, UNIT_BLK, 2, BLOCK])
        x_bank = [score_bank[0][:].rearrange("p a b -> p (a b)"), score_bank[1][:].rearrange("p a b -> p (a b)"),
                  turn_bank[0][:], turn_bank[1][:]]

        ctx_a.close()
        wo_raw = sb_b("wo_raw", [P, WO_RAW, D_MODEL])
        wo_early = sb_b("wo_early", [P, WO_EARLY, 2, D_MODEL], F32R)
        mix_hi = sb_b("mix_hi", [P, 2, MIX_KT, P], F32R)
        mix_lo = sb_b("mix_lo", [P, 2, MIX_KT, P], F32R)
        sb_b("pad", [P, D_MODEL])
        mix_raw = sb_b("mix_raw", [P, 2, MIX_KT, P])
        wo_late = sb_b("wo_late", [P, MIX_KT - WO_EARLY, 2, D_MODEL], F32R)
        z = sb_b("z", [P, 2, D_MODEL])
        gain_final = sb_b("gain_final", [P, D_MODEL])
        ctx.callback(ctx_b.close)

        def wo_part(kt, part):
            return wo_early[:, kt, part, :] if kt < WO_EARLY else wo_late[:, kt - WO_EARLY, part, :]

        flat_out = out_bank[:].rearrange("p a h q -> p (a h q)")
        all_banks = [b[:] for b in job_bank] + x_bank + [flat_out]
        mix_bank = [[all_banks[4 * p + 2 * s:4 * p + 2 * s + 2] for s in range(2)] for p in range(2)]

        gain_landed = sem("gain_landed")
        wo_landed = sems("wo_landed", WO_RAW)
        wo_hi_ready = sem("wo_hi_ready")
        wo_ready = sem("wo_ready")
        mix_landed = sems("mix_landed", 2)
        mix_hi_ready = sem("mix_hi_ready")
        mix_ready = sem("mix_ready")
        res_landed = sems("res_landed", 2)
        mix_var = sem("mix_var")
        mix_rooted = sem("mix_rooted")
        tile_done = sem("tile_done")
        z_ready = sem("z_ready")
        z_squared = sem("z_squared")
        z_var = sem("z_var")
        z_rooted = sem("z_rooted")
        y_ready = sem("y_ready")
        y_stored = sems("y_stored", 2)

        consts_landed = sem("consts_landed")
        pool_set = sem("pool_set")
        bias_set = sem("bias_set")
        x_first_landed = sems("x_first_landed", XT)
        x_landed = sems("x_landed", 2)
        x_squared = sem("x_squared")
        x_rooted = sem("x_rooted")
        x_var = sem("x_var")
        x_scaled = sem("x_scaled")
        x_turned = sem("x_turned")
        h_hi_ready = sem("h_hi_ready")
        h_ready = sem("h_ready")
        w_landed = sems("w_landed", RING)
        w_hi_ready = sem("w_hi_ready")
        w_ready = sem("w_ready")
        job_done = sem("job_done")
        evacuated = sems("evacuated", RING)
        k_hi_ready = sem("k_hi_ready")
        k_ready = sem("k_ready")
        v_turned = sem("v_turned")
        v_hi_ready = sem("v_hi_ready")
        v_ready = sem("v_ready")
        q_hi_ready = sem("q_hi_ready")
        scores_done = sem("scores_done")
        scores_read = sem("scores_read")
        unit_begun = sem("unit_begun")
        max_ready = sem("max_ready")
        exp_done = sem("exp_done")
        rinv_ready = sem("rinv_ready")
        probs_ready = sem("probs_ready")
        probs_turned = sem("probs_turned")
        masked = sem("masked")
        pT_hi_ready = sem("pT_hi_ready")
        pT_ready = sem("pT_ready")
        pv_done = sem("pv_done")
        shifted = sem("shifted")
        attn_ready = sem("attn_ready")
        tanh_ready = sem("tanh_ready")
        gated_ready = sem("gated_ready")
        stored = sems("stored", CHUNKS)
        squares_step = sem("squares_step")
        dve_step = sem("dve_step")
        mix_summed = sem("mix_summed")
        mix_read = sem("mix_read")

        def job_no(hf, it, j, ch):
            return hf * HALF_JOBS + KV_JOBS + ITER_JOBS * it + JOB_ORDER.index((j, ch))

        def kv_job_no(hf, tile, ch):
            return hf * HALF_JOBS + KV_ORDER.index((tile, ch))

        def bank_use(hf, it, j, ch):
            k = JOB_ORDER.index((j, ch))
            return BANK_USE["last", hf, k] if isinstance(it, int) else BANK_USE["tiles", hf] + k

        def job_slot(hf, it, j, ch):
            return bank_use(hf, it, j, ch) % RING

        def evac_count(hf, it, j, ch):
            count = bank_use(hf, it, j, ch) // RING + 1
            return count if isinstance(it, int) else count + ITER_JOBS // RING * it

        def tile_slot(hf, j):
            return (hf * HALF_TILES + 2 + j) % RING

        def tile_no(hf, it, j):
            return hf * HALF_TILES + 2 + TILE_JOBS * it + j

        def landed_count(hf, it, j):
            return 16 * ((hf * HALF_TILES + 2 + j) // RING + 1) + 16 * (TILE_JOBS // RING) * it

        def unit_no(hf, it, u):
            return hf * UNITS * TILES + u + UNITS * it

        def squares_count(hf, it):
            return hf + 1 + SQUARE_STEPS * (hf * TILES + it)

        def gated_count(hf, it, k):
            return 2 * CHUNKS * (hf * TILES + it) + k + 1

        def tiles_of_half(eng, run):
            with eng.Fori(0, PER_KV) as i4:
                run(i4 + 0, 0, i4)
            with eng.Fori(0, PER_KV - 1) as i4:
                run(PER_KV + i4, 1, i4)
            run(TILES - 1, 1, 0)

        def tiles_of_tokens(eng, run):
            run(0, 0)
            run(1, 1)
            with eng.Fori(1, TT // 2 - 1) as t2:
                run(0, 2 * t2)
                run(1, 2 * t2 + 1)
            run(0, TT - 2)
            run(1, TT - 1)

        def x_turn_bank(hf, t, c):
            if hf == 1 and t < len(X_AFTER):
                return job_bank[BANK_USE["x", t, c] % RING][:]
            return x_bank[2 * ((t + hf) % 2) + c]

        def h_count(hf, t):
            return 2 * (hf * (XT - len(X_AFTER)) + t + 1)

        block = ctx.enter_context(nc.Block())

        @block.sync
        def _(sp):
            def load_first_x(t):
                sp.dma_start(x_first[t], x[t * P:(t + 1) * P, :]).then_inc(x_first_landed[t], 16)

            def load_x(t, load):
                if load < 2:
                    sp.wait_ge(x_turned, 2 * XT)
                elif load < XT + 2:
                    sp.wait_ge(x_squared, XT + load - 1)
                else:
                    sp.wait_ge(x_turned, 2 * (load - 1))
                sp.dma_start(x_sb[:, load % 2, :], x[(XT + t) * P:(XT + t + 1) * P, :]
                             ).then_inc(x_landed[load % 2], 16)

            def load_w(n):
                if n >= RING:
                    sp.wait_ge(w_ready, n - RING + 1)
                sp.dma_start(w_raw[:, n % RING, :, :].rearrange("p k c -> p (k c)"), w_in[n % HALF_TILES]
                             ).then_inc(w_landed[n % RING], 16)

            load_first_x(0)
            sp.dma_start(gain_in[:], norm_in.to_broadcast([P, D_MODEL])).then_inc(gain_landed, 16)
            load_first_x(1)
            load_first_x(2)
            load_w(0)
            load_first_x(3)
            load_w(1)
            for t in range(4, XT):
                load_first_x(t)
            sp.dma_start(sink_bc[:], sinks.to_broadcast([P, HEADS])).then_inc(consts_landed, 16)
            sp.dma_start(conv_sb[:], conv_w).then_inc(consts_landed, 16)
            sp.dma_start(gains[:, 0, :], gain_conv).then_inc(consts_landed, 16)
            sp.dma_start(gains[:, 1, :], gain_attn).then_inc(consts_landed, 16)
            sp.wait_ge(bias_set, 1)
            load_w(2)
            for hf in range(HALVES):
                for n in range(LOAD_AHEAD, 2 + LOAD_AHEAD):
                    load_w(hf * HALF_TILES + n)

                def tile(it, g, i4):
                    last = isinstance(it, int)
                    if last and hf == 0:
                        load_x(0, 0)
                        load_x(1, 1)
                    for j in range(TILE_JOBS):
                        if last and hf == 1 and j + LOAD_AHEAD >= TILE_JOBS:
                            break
                        slot = tile_slot(hf, j + LOAD_AHEAD)
                        sp.wait_ge(w_ready, tile_no(hf, it, j + LOAD_AHEAD) - RING + 1)
                        source = 2 + LOAD_AHEAD + TILE_JOBS * it + j
                        sp.dma_start(w_raw[:, slot, :, :].rearrange("p k c -> p (k c)"),
                                     w_in[source % HALF_TILES if last else source]).then_inc(w_landed[slot], 16)
                        if last and hf == 0:
                            for t in range(2 + 2 * j, 4 + 2 * j) if j < 3 else ():
                                load_x(t, t)
                            if j == 3:
                                load_x(0, XT)
                                load_x(1, XT + 1)
                    if last and hf == 1:
                        for kt in range(WO_RAW):
                            load_wo(kt)
                    for k in range(2 * CHUNKS):
                        for t in {1: (2,), 2: (3,), 3: (4, 5, 6)}.get(k, ()) if last and hf == 0 else ():
                            load_x(t, XT + t)
                        sp.wait_ge(gated_ready, gated_count(hf, it, k))
                        ch, branch = k // 2, k % 2
                        t0 = (hf * CHUNKS + ch) * (CHUNK // P)
                        sp.dma_start(mixed_dram[t0:t0 + CHUNK // P, :, TILES * branch + it, :].rearrange(
                            "t p c -> p t c"), gated[:, ch, :].rearrange("p (t c) -> p t c", c=P)
                            ).then_inc(stored[ch], 16)
                        if last and hf == 1 and k == 0:
                            for ch in range(CHUNKS):
                                sp.wait_ge(stored[ch], 16 * (2 * TILES + 1))
                            load_mix(0, 0)
                            sp.wait_ge(scores_done, unit_no(HALVES, 0, 0))
                            load_mix(1, 1)
                    if last and hf == 0:
                        load_x(XT - 1, 2 * XT - 1)

                def load_wo(kt):
                    if kt == 0:
                        sp.wait_ge(x_turned, 2 * TT)
                    if kt >= WO_RAW:
                        sp.wait_ge(wo_ready, kt - WO_RAW + 1)
                    sp.dma_start(wo_raw[:, kt % WO_RAW, :], w_out[kt]).then_inc(wo_landed[kt % WO_RAW], 16)

                def load_mix(p, t):
                    sp.dma_start(mix_raw[:, p].rearrange("q k c -> q (k c)"),
                                 mixed_dram[t].rearrange("q k c -> q (k c)")).then_inc(mix_landed[p], 16)

                def load_residual(p, t):
                    sp.dma_start(z[:, p, :], x[bass.ts(t, P), :]).then_inc(res_landed[p], 16)

                tiles_of_half(sp, tile)
            for kt in range(WO_RAW, MIX_KT):
                load_wo(kt)
                if kt == WO_EARLY:
                    for ch in range(CHUNKS):
                        sp.wait_ge(stored[ch], 16 * (2 * HALVES * TILES + 1))
                    sp.wait_ge(mix_summed, HALVES)
                    load_residual(0, 0)
                    load_residual(1, 1)
                    sp.dma_start(gain_final[:], norm_final.to_broadcast([P, D_MODEL])).then_inc(gain_landed, 16)
            with sp.Fori(1, TT // 2) as t2:
                for p in range(2):
                    sp.wait_ge(mix_ready, 2 * t2 + p - 1)
                    load_mix(p, 2 * t2 + p)
                    sp.wait_ge(y_stored[p], 16 * t2)
                    load_residual(p, 2 * t2 + p)

        @block.gpsimd
        def _(pool):
            nc.gpsimd.memset(in_block[:], 1.0)
            nc.gpsimd.memset(ident[:], 0.0).then_inc(pool_set, 1)
            nc.gpsimd.memset(ones[:], 1.0)
            nc.gpsimd.memset(cu_halo[:], 0.0)
            nc.gpsimd.memset(keys[:, :, :, 0:BLOCK].bitcast(F32), 0.0)
            nc.gpsimd.memset(vals[:, 0, :, :, :].bitcast(F32), 0.0)
            nc.gpsimd.iota(dist, pattern=[[-1, 2 * BLOCK]], base=BLOCK, channel_multiplier=1)
            pool.wait_ge(pool_set, 1)
            nc.gpsimd.affine_select(out=ident[:], in_=ident[:], compare_op=ALU.not_equal, fill=1.0, base=0,
                                    pattern=[[-1, P]], channel_multiplier=1).then_inc(pool_set, 1)
            nc.gpsimd.affine_select(out=in_block[:, 0], in_=in_block[:, 0], compare_op=ALU.is_ge, fill=0.0, base=-1,
                                    pattern=[[-1, BLOCK]], channel_multiplier=1)
            nc.gpsimd.affine_select(out=in_block[:, 1], in_=in_block[:, 1], compare_op=ALU.is_ge, fill=0.0, base=0,
                                    pattern=[[1, BLOCK]], channel_multiplier=-1)
            pool.wait_ge(bias_set, 1)
            nc.gpsimd.affine_select(out=bias[:], in_=bias[:], compare_op=ALU.is_ge, fill=MASKED, base=BLOCK,
                                    pattern=[[0, 2], [0, 2], [-1, 2 * BLOCK]], channel_multiplier=1
                                    ).then_inc(bias_set, 1)
            pool.wait_ge(bias_set, 2)
            nc.gpsimd.affine_select(out=bias[:], in_=bias[:], compare_op=ALU.is_ge, fill=MASKED, base=-1,
                                    pattern=[[0, 2], [0, 2], [1, 2 * BLOCK]], channel_multiplier=-1
                                    ).then_inc(bias_set, 1)
            pool.wait_ge(bias_set, 3)
            nc.gpsimd.affine_select(out=bias[:, 1], in_=bias[:, 1], compare_op=ALU.is_ge, fill=MASKED,
                                    base=-BLOCK, pattern=[[0, 2], [1, 2 * BLOCK]], channel_multiplier=0
                                    ).then_inc(bias_set, 1)

            for hf in range(HALVES):
                if hf > 0:
                    pool.wait_ge(mix_summed, hf)
                nc.gpsimd.memset(ssq_conv[:], 0.0)
                nc.gpsimd.memset(ssq_attn[:], 0.0).then_inc(squares_step, 1)

                def tile(it, g, i4):
                    def normalise(u):
                        pool.wait_ge(rinv_ready, unit_no(hf, it, u) + 1)
                        merged = probs[:, u % 2].rearrange("p h b k -> p (h b) k")[:, :, 0:BLOCK]
                        nc.gpsimd.tensor_tensor(
                            merged, merged, smax[:, u % 2, ROWSUM, :].unsqueeze(2).to_broadcast([P, 4, BLOCK]),
                            ALU.mult).then_inc(probs_ready, 1)

                    def add_squares(src, total, ch, k):
                        pool.wait_ge(squares_step, squares_count(hf, it) + 2 * k)
                        nc.gpsimd.tensor_tensor(square[:], src[:, ch, :], src[:, ch, :],
                                                ALU.mult).then_inc(squares_step, 1)
                        pool.wait_ge(squares_step, squares_count(hf, it) + 2 * k + 1)
                        nc.gpsimd.tensor_tensor(total[:, ch, :], total[:, ch, :], square[:],
                                                ALU.add).then_inc(squares_step, 1)

                    normalise(0)
                    normalise(1)
                    normalise(2)
                    pool.wait_ge(evacuated[job_slot(hf, it, B, 0)], evac_count(hf, it, B, 0))
                    add_squares(conv_y, ssq_conv, 0, 0)
                    normalise(3)
                    pool.wait_ge(attn_ready, unit_no(hf, it, 1) + 2)
                    add_squares(attn_y, ssq_attn, 0, 1)
                    pool.wait_ge(evacuated[job_slot(hf, it, B, 1)], evac_count(hf, it, B, 1))
                    add_squares(conv_y, ssq_conv, 1, 2)
                    pool.wait_ge(attn_ready, unit_no(hf, it, 3) + 2)
                    add_squares(attn_y, ssq_attn, 1, 3)

                tiles_of_half(pool, tile)

            with pool.Fori(0, TT // 2) as t2:
                for p in range(2):
                    pool.wait_ge(y_ready, 2 * t2 + p + 1)
                    pool.dma_start(out[bass.ts(2 * t2 + p, P), :], z[:, p, :]).then_inc(y_stored[p], 16)
            for p in range(2):
                pool.wait_ge(y_stored[p], 16 * (TT // 2))

        @block.scalar
        def _(act):
            def split_w(slot, landed, used):
                act.wait_ge(w_landed[slot], landed)
                if used is not None:
                    act.wait_ge(job_done, used)
                nc.scalar.activation(w_hi[:, slot], w_raw[:, slot], ACT.Copy).then_inc(w_hi_ready, 1)

            def square_x(n, source, junk):
                nc.scalar.activation(junk, source, ACT.Square, accum_out=x_stat[:, n % XT, 0:1]
                                     ).then_inc(x_squared, 1)

            def h_hi(hf, t):
                n = hf * XT + t
                for c in range(2):
                    act.wait_ge(x_turned, 2 * n + c + 1)
                    nc.scalar.activation(hT_hi[:, 4 * c:4 * c + 4, t * P:(t + 1) * P],
                                         x_turn_bank(hf, t, c).rearrange("p (k c) -> p k c", c=P),
                                         ACT.Copy).then_inc(h_hi_ready, 1)

            def k_hi(hf, ch):
                slot = BANK_USE["kv", hf, 0, ch] % RING
                cols = slice((1 + 4 * ch) * BLOCK, (5 + 4 * ch) * BLOCK)
                act.wait_ge(job_done, kv_job_no(hf, 0, ch) + 1)
                if hf > 0 and ch == 0:
                    act.wait_ge(k_ready, (CHUNKS + 1) * hf)
                for g in range(KV_HEADS):
                    rows = slice(HD * g, HD * g + HD)
                    other = slice(HD * (1 - g), HD * (1 - g) + HD)
                    nc.scalar.activation(keys[rows, g, 0, cols], job_bank[slot][rows, :], ACT.Copy)
                    ins = nc.scalar.activation(keys[other, g, 0, cols], job_bank[slot][rows, :], ACT.Copy)
                ins.then_inc(k_hi_ready, 1)

            def v_copy(hf, ch):
                slot = BANK_USE["kv", hf, 1, ch] % RING
                act.wait_ge(job_done, kv_job_no(hf, 1, ch) + 1)
                nc.scalar.activation(vT[:, ch, :], job_bank[slot][:], ACT.Copy).then_inc(evacuated[slot], 1)

            def split_w_static(n, used=None):
                split_w(n % RING, 16 * (n // RING + 1), used)

            def round_mix(p, t, wait):
                act.wait_ge(mix_landed[p], 8 * (t - p) + 16)
                if wait:
                    act.wait_ge(tile_done, t - 1)
                nc.scalar.activation(mix_hi[:, p], mix_raw[:, p], ACT.Copy).then_inc(mix_hi_ready, 1)

            def round_wo(kt):
                act.wait_ge(wo_landed[kt % WO_RAW], 16 * (kt // WO_RAW + 1))
                nc.scalar.activation(wo_part(kt, 0), wo_raw[:, kt % WO_RAW, :], ACT.Copy).then_inc(wo_hi_ready, 1)

            junk = attn_y[:].rearrange("p a b -> p (a b)")
            for hf in range(HALVES):
                if hf == 0:
                    def squares(tiles):
                        for t in tiles:
                            act.wait_ge(x_first_landed[t], 16)
                            if t >= 1:
                                act.wait_ge(x_squared, t)
                            square_x(t, x_first[t], junk)

                    def root(i, t, count):
                        act.wait_ge(x_var, i + 1)
                        nc.scalar.activation(x_stat[:, t:t + count, 2:3], x_stat[:, t:t + count, 1:2], ACT.Sqrt
                                             ).then_inc(x_rooted, 1)

                    for i, (t, count) in enumerate(STAT_GROUPS):
                        if i == 3:
                            h_hi(0, 2)
                            h_hi(0, 3)
                        squares(range(t, t + count))
                        root(i, t, count)
                        if i == 2:
                            split_w_static(0)
                            h_hi(0, 0)
                            h_hi(0, 1)
                            split_w_static(1)
                    h_hi(0, 4)
                    h_hi(0, 5)
                    k_hi(0, 0)
                    v_copy(0, 0)
                    h_hi(0, 6)
                    h_hi(0, 7)
                    split_w_static(2)
                else:
                    h_hi(1, 4)
                    k_hi(1, 0)
                    h_hi(1, 5)
                    h_hi(1, 6)
                    split_w_static(HALF_TILES + 2, HALF_JOBS)
                    v_copy(1, 0)
                    h_hi(1, 7)
                k_hi(hf, 1)
                split_w_static(hf * HALF_TILES + 3, kv_job_no(hf, 0, 1) + 1)
                v_copy(hf, 1)
                for ch in range(CHUNKS):
                    act.wait_ge(v_turned, hf * CHUNKS + ch + 1)
                    nc.scalar.activation(vals[:, 1 + 4 * ch:5 + 4 * ch, :, 0, :],
                                         turn_bank[ch][:].rearrange("p (b g d) -> p b g d", g=KV_HEADS, d=HD),
                                         ACT.Copy).then_inc(v_hi_ready, 1)

                def tile(it, g, i4):
                    last = isinstance(it, int)

                    def split_next(j):
                        if last and hf == HALVES - 1 and j + AHEAD >= TILE_JOBS:
                            return
                        used = {0: -1, 1: JOB_ORDER.index((Q, 1)), 2: JOB_ORDER.index((C, 1)),
                                3: JOB_ORDER.index((U, 1)), 4: JOB_ORDER.index((B, 1)),
                                5: JOB_ORDER.index((GC, 1))}[j]
                        split_w(tile_slot(hf, j + AHEAD), landed_count(hf, it, j + AHEAD),
                                job_no(hf, it, Q, 0) + used + 1)

                    def q_hi(ch):
                        act.wait_ge(job_done, job_no(hf, it, Q, ch) + 1)
                        bank = job_bank[job_slot(hf, it, Q, ch)]
                        cols = slice(ch * CHUNK, (ch + 1) * CHUNK)
                        nc.scalar.activation(qs[0:HD, 0, cols], bank[0:HD, :], ACT.Copy, scale=QSCALE)
                        nc.scalar.activation(qs[HD:P, 1, cols], bank[HD:P, :], ACT.Copy, scale=QSCALE
                                             ).then_inc(q_hi_ready, 1)

                    def copy_c(ch):
                        act.wait_ge(job_done, job_no(hf, it, C, ch) + 1)
                        slot = job_slot(hf, it, C, ch)
                        nc.scalar.activation(c_sb[:, ch, :], job_bank[slot][:], ACT.Copy).then_inc(evacuated[slot], 1)

                    def exps(u):
                        act.wait_ge(max_ready, unit_no(hf, it, u) + 1)
                        for c in range(4):
                            nc.scalar.activation(probs[:, u % 2, c // 2, c % 2, 0:BLOCK],
                                                 probs[:, u % 2, c // 2, c % 2, 0:BLOCK], ACT.Exp,
                                                 bias=smax[:, u % 2, NEGMAX, c:c + 1],
                                                 accum_out=smax[:, u % 2, ROWSUM, c:c + 1])
                        nc.scalar.activation(smax[:, u % 2, SINKEXP, :], smax[:, u % 2, SINKDIFF, :],
                                             ACT.Exp).then_inc(exp_done, 1)

                    def pT_round(u):
                        act.wait_ge(pv_done, unit_no(hf, it, u) + 1)
                        for b in range(UNIT_BLK):
                            act.wait_ge(masked, 2 * unit_no(hf, it, u) + b + 1)
                            nc.scalar.activation(pT_hi[:, b, :], parted[:, u % 2, b].rearrange("p k h q -> p (k h q)"),
                                                 ACT.Copy).then_inc(pT_hi_ready, 1)

                    def shift(u):
                        act.wait_ge(attn_ready, unit_no(hf, it, u) + 1)
                        act.wait_ge(pv_done, unit_no(hf, it, u) + 2)
                        nc.scalar.activation(o_shift[0:HD], out_bank[HD:P, :, 0, :], ACT.Copy)
                        nc.scalar.activation(o_shift[HD:P], out_bank[0:HD, :, 1, :], ACT.Copy).then_inc(shifted, 1)

                    def tanh_gate(j, ch):
                        if j == GC:
                            act.wait_ge(evacuated[job_slot(hf, it, B, ch)], evac_count(hf, it, B, ch))
                        else:
                            act.wait_ge(gated_ready, gated_count(hf, it, 2 * ch))
                        act.wait_ge(job_done, job_no(hf, it, j, ch) + 1)
                        nc.scalar.activation(tanh_sb[:, ch, :], job_bank[job_slot(hf, it, j, ch)][:], ACT.Tanh,
                                             scale=0.5).then_inc(tanh_ready, 1)

                    ahead = last and hf == 0

                    def square_next(*tokens):
                        for t in tokens if ahead else ():
                            act.wait_ge(x_landed[t % 2], 16 * (t // 2 + 1))
                            square_x(XT + t, x_sb[:, t % 2, :], x_sb[:, t % 2, :])

                    q_hi(0)
                    square_next(0, 1)
                    split_next(0)
                    q_hi(1)
                    split_next(1)
                    exps(0)
                    copy_c(0)
                    square_next(2, 3)
                    copy_c(1)
                    split_next(2)
                    exps(1)
                    square_next(4, 5, 6, 7)
                    pT_round(0)
                    split_next(3)
                    exps(2)
                    if ahead:
                        act.wait_ge(x_var, len(STAT_GROUPS) + 1)
                        nc.scalar.activation(x_stat[:, :, 2:3], x_stat[:, :, 1:2], ACT.Sqrt).then_inc(x_rooted, 1)
                    shift(0)
                    pT_round(1)
                    tanh_gate(GC, 0)
                    if ahead:
                        tanh_gate(GA, 0)
                        h_hi(1, 0)
                    exps(3)
                    if not ahead:
                        tanh_gate(GA, 0)
                    shift(1)
                    pT_round(2)
                    split_next(4)
                    if ahead:
                        h_hi(1, 1)
                    tanh_gate(GC, 1)
                    split_next(5)
                    if ahead:
                        h_hi(1, 2)
                    shift(2)
                    pT_round(3)
                    if ahead:
                        h_hi(1, 3)
                    if last and hf == HALVES - 1:
                        act.wait_ge(job_done, job_no(hf, it, GC, 1) + 1)
                        round_mix(0, 0, False)
                    tanh_gate(GA, 1)
                    if last and hf == HALVES - 1:
                        act.wait_ge(job_done, HALVES * HALF_JOBS)
                        round_wo(0)
                    shift(3)

                tiles_of_half(act, tile)

            def finish(p, t):
                first, final = isinstance(t, int) and t == 0, isinstance(t, int) and t == TT - 1
                if first:
                    act.wait_ge(mix_var, 1)
                    nc.scalar.activation(mix_root[:], mix_ssq[:], ACT.Sqrt).then_inc(mix_rooted, 1)
                    round_mix(0, 2, True)
                elif not final and not (isinstance(t, int) and t == 1):
                    round_mix(1 - p, t + 1, True)
                act.wait_ge(z_ready, t + 1)
                nc.scalar.activation(wo_raw[:, 0, :], z[:, p, :], ACT.Square, accum_out=z_stat[:, p, 0:1]
                                     ).then_inc(z_squared, 1)
                act.wait_ge(z_var, t + 1)
                nc.scalar.activation(z_stat[:, p, 2:3], z_stat[:, p, 1:2], ACT.Sqrt).then_inc(z_rooted, 1)

            for kt in range(1, MIX_KT):
                if kt == GROUP_KT:
                    round_mix(1, 1, False)
                if kt == WO_EARLY:
                    act.wait_ge(mix_summed, HALVES)
                    for ch in range(CHUNKS):
                        act.wait_ge(stored[ch], 16 * (2 * HALVES * TILES + 1))
                round_wo(kt)
            tiles_of_tokens(act, finish)

        @block.vector
        def _(dve):
            steps = [0]

            def link(ins):
                steps[0] += 1
                ins.then_inc(dve_step, 1)
                dve.wait_ge(dve_step, steps[0])

            def split_w(n, slot):
                dve.wait_ge(w_hi_ready, n + 1)
                nc.vector.tensor_tensor(w_lo[:, slot], w_raw[:, slot], w_hi[:, slot].bitcast(F32),
                                        ALU.subtract).then_inc(w_ready, 1)

            def newton(step, r, root, var):
                step(nc.vector.reciprocal(r, root))
                step(nc.vector.tensor_tensor(root, r, r, ALU.mult))
                step(nc.vector.tensor_tensor(root, root, var, ALU.mult))
                step(nc.vector.tensor_scalar(root, root, -0.5, 1.5, ALU.mult, ALU.add))
                step(nc.vector.tensor_tensor(r, r, root, ALU.mult))

            def variance(t, n, count):
                dve.wait_ge(x_squared, n)
                nc.vector.tensor_scalar(x_stat[:, t:t + count, 1:2], x_stat[:, t:t + count, 0:1],
                                        1.0 / D_MODEL, EPS, ALU.mult, ALU.add).then_inc(x_var, 1)

            def x_root(t, n, count):
                dve.wait_ge(x_rooted, n)
                newton(link, *(x_stat[:, t:t + count, i:i + 1] for i in (3, 2, 1)))

            def scale_x(hf, t):
                tokens = x_first[t] if hf == 0 else x_sb[:, t % 2, :]
                if hf > 0:
                    dve.wait_ge(x_landed[t % 2], 16 * ((XT + t) // 2 + 1))
                nc.vector.scalar_tensor_tensor(out=tokens, in0=tokens, scalar=x_stat[:, t, 3:4], in1=gain_in[:],
                                               op0=ALU.mult, op1=ALU.mult).then_inc(x_scaled, 1)

            def h_lo(hf, t):
                n = hf * XT + t
                for c in range(2):
                    dve.wait_ge(h_hi_ready, 2 * n + c + 1)
                    ins = nc.vector.tensor_tensor(hT_lo[:, 4 * c:4 * c + 4, t * P:(t + 1) * P],
                                                  x_turn_bank(hf, t, c).rearrange("p (k c) -> p k c", c=P),
                                                  hT_hi[:, 4 * c:4 * c + 4, t * P:(t + 1) * P].bitcast(F32),
                                                  ALU.subtract)
                    in_job_bank = hf == 1 and t < len(X_AFTER)
                    ins.then_inc(evacuated[BANK_USE["x", t, c] % RING] if in_job_bank else h_ready, 1)

            def k_lo(hf, ch):
                use = BANK_USE["kv", hf, 0, ch]
                cols = slice((1 + 4 * ch) * BLOCK, (5 + 4 * ch) * BLOCK)
                dve.wait_ge(k_hi_ready, hf * CHUNKS + ch + 1)
                for g in range(KV_HEADS):
                    rows = slice(HD * g, HD * g + HD)
                    ins = nc.vector.tensor_tensor(keys[rows, g, 1, cols], job_bank[use % RING][rows, :],
                                                  keys[rows, g, 0, cols].bitcast(F32), ALU.subtract)
                ins.then_inc(evacuated[use % RING], 1)
                dve.wait_ge(evacuated[use % RING], use // RING + 1)
                for g in range(KV_HEADS):
                    rows = slice(HD * g, HD * g + HD)
                    other = slice(HD * (1 - g), HD * (1 - g) + HD)
                    ins = nc.vector.tensor_copy(keys[other, g, 1, cols], keys[rows, g, 1, cols].bitcast(F32))
                ins.then_inc(k_ready, 1)

            def mix_rest(p, t):
                dve.wait_ge(mix_hi_ready, t + 1)
                nc.vector.tensor_tensor(mix_lo[:, p], mix_raw[:, p], mix_hi[:, p].bitcast(F32), ALU.subtract
                                        ).then_inc(mix_ready, 1)

            def wo_rest(kt):
                dve.wait_ge(wo_hi_ready, kt + 1)
                nc.vector.tensor_tensor(wo_part(kt, 1), wo_raw[:, kt % WO_RAW, :], wo_part(kt, 0).bitcast(F32),
                                        ALU.subtract).then_inc(wo_ready, 1)

            dve.sem_inc(scores_read, 1)
            dve.sem_inc(pT_ready, 2)
            dve.sem_inc(attn_ready, 1)
            for ch in range(CHUNKS):
                dve.sem_inc(stored[ch], 16)
            dve.wait_ge(gain_landed, 16)
            for hf in range(HALVES):
                if hf == 0:
                    def prepare(i):
                        t, count = STAT_GROUPS[i]
                        variance(t, t + count, count)
                        x_root(t, i + 1, count)

                    prepare(0)
                    scale_x(0, 0)
                    prepare(1)
                    scale_x(0, 1)
                    prepare(2)
                    scale_x(0, 2)
                    h_lo(0, 0)
                    scale_x(0, 3)
                    h_lo(0, 1)
                    split_w(0, 0)
                    h_lo(0, 2)
                    h_lo(0, 3)
                    split_w(1, 1)
                    prepare(3)
                    scale_x(0, 4)
                    scale_x(0, 5)
                    scale_x(0, 6)
                    h_lo(0, 4)
                    scale_x(0, 7)
                    h_lo(0, 5)
                    dve.wait_ge(pool_set, 2)
                    for h in range(2):
                        for first in range(2):
                            ins = nc.vector.tensor_scalar(
                                bias[:, first, h, :], dist.rearrange("p a b -> p (a b)"),
                                -(2.0 ** (-8.0 * (h + 1) / HEADS)), None, ALU.mult)
                    ins.then_inc(bias_set, 1)
                    k_lo(0, 0)
                    dve.wait_ge(consts_landed, 16 * 4)
                    link(nc.vector.tensor_scalar(gains[:], gains[:], 0.5, None, ALU.mult))
                    h_lo(0, 6)
                    h_lo(0, 7)
                    split_w(2, 2)
                else:
                    dve.wait_ge(pv_done, unit_no(hf, 0, 0) + 1)
                    nc.vector.tensor_copy(keys[:, :, :, 0:BLOCK], keys[:, :, :, HBLK * BLOCK:].bitcast(F32))
                    nc.vector.tensor_copy(vals[:, 0], vals[:, HBLK].bitcast(F32)).then_inc(k_ready, 1)
                    h_lo(1, 4)
                    scale_x(1, 6)
                    k_lo(1, 0)
                    h_lo(1, 5)
                    split_w(HALF_TILES + 2, (HALF_TILES + 2) % RING)
                    h_lo(1, 6)
                    scale_x(1, 7)
                    h_lo(1, 7)
                    link(nc.vector.tensor_scalar(bias[:], bias[:], 2.0 ** TILES, None, ALU.mult))
                k_lo(hf, 1)
                split_w(hf * HALF_TILES + 3, (hf * HALF_TILES + 3) % RING)
                for ch in range(CHUNKS):
                    dve.wait_ge(v_hi_ready, hf * CHUNKS + ch + 1)
                    nc.vector.tensor_tensor(vals[:, 1 + 4 * ch:5 + 4 * ch, :, 1, :],
                                            turn_bank[ch][:].rearrange("p (b g d) -> p b g d", g=KV_HEADS, d=HD),
                                            vals[:, 1 + 4 * ch:5 + 4 * ch, :, 0, :].bitcast(F32),
                                            ALU.subtract).then_inc(v_ready, 1)
                if hf > 0:
                    dve.wait_ge(mix_summed, hf)
                    nc.vector.tensor_copy(mix_ssq[:, :, (hf - 1) * XT:hf * XT],
                                          flat_out[:, 0:2 * XT].rearrange("p (s t) -> p s t", s=2)
                                          ).then_inc(mix_read, 1)

                def tile(it, g, i4):
                    last = isinstance(it, int)
                    base = steps[0]
                    k = [0]

                    def step(ins):
                        k[0] += 1
                        ins.then_inc(dve_step, 1)
                        dve.wait_ge(dve_step, base + k[0] + VECTOR_STEPS * i4)

                    def split_next(j):
                        if not (last and hf == HALVES - 1 and j + AHEAD >= TILE_JOBS):
                            split_w(tile_no(hf, it, j + AHEAD), tile_slot(hf, j + AHEAD))

                    def q_lo(ch):
                        dve.wait_ge(q_hi_ready, CHUNKS * (hf * TILES + it) + ch + 1)
                        slot = job_slot(hf, it, Q, ch)
                        bank = job_bank[slot]
                        cols = slice(ch * CHUNK, (ch + 1) * CHUNK)
                        nc.vector.scalar_tensor_tensor(out=qs[HD:P, 0, cols], in0=bank[0:HD, :], scalar=QSCALE,
                                                       in1=qs[0:HD, 0, cols].bitcast(F32),
                                                       op0=ALU.mult, op1=ALU.subtract)
                        nc.vector.scalar_tensor_tensor(out=qs[0:HD, 1, cols], in0=bank[HD:P, :], scalar=QSCALE,
                                                       in1=qs[HD:P, 1, cols].bitcast(F32),
                                                       op0=ALU.mult, op1=ALU.subtract).then_inc(evacuated[slot], 1)

                    def maxima(u):
                        dve.wait_ge(bias_set, 4)
                        dve.wait_ge(scores_done, unit_no(hf, it, u) + 1)
                        dve.wait_ge(probs_turned, unit_no(hf, it, u) + 1)
                        dve.wait_ge(pT_ready, 2 * unit_no(hf, it, u) + (2 if u == 0 else 0))
                        dve.sem_inc(unit_begun, 1)
                        st = smax[:, u % 2]
                        for c in range(4):
                            h, b = c // 2, c % 2
                            first = 1 if (hf == 0 and u == 0 and b == 0) else 0
                            ins = nc.vector.tensor_tensor_reduce(
                                probs[:, u % 2, h, b, :], score_bank[h][:, b, :], bias[:, first, h, :], 1.0,
                                MASKED, ALU.add, ALU.max, st[:, ROWMAX, c:c + 1])
                        ins.then_inc(scores_read, 1)
                        dve.wait_ge(scores_read, unit_no(hf, it, u) + 2)
                        nc.vector.tensor_tensor(probs[:, u % 2, :, :, 0:BLOCK], probs[:, u % 2, :, :, 0:BLOCK],
                                                probs[:, u % 2, :, :, BLOCK:], ALU.max)
                        step(nc.vector.tensor_tensor(st[:, MAX, :], st[:, ROWMAX, :],
                                                     sink_now[:].rearrange("p h b -> p (h b)"), ALU.max))
                        nc.vector.tensor_scalar(st[:, NEGMAX, :], st[:, MAX, :], -1.0, None, ALU.mult)
                        nc.vector.tensor_tensor(st[:, SINKDIFF, :], sink_now[:].rearrange("p h b -> p (h b)"),
                                                st[:, MAX, :], ALU.subtract).then_inc(max_ready, 1)

                    def denominators(u):
                        st = smax[:, u % 2]
                        dve.wait_ge(exp_done, unit_no(hf, it, u) + 1)
                        step(nc.vector.tensor_tensor(st[:, SINKEXP, :], st[:, SINKEXP, :], st[:, ROWSUM, :],
                                                     ALU.add))
                        nc.vector.reciprocal(st[:, ROWSUM, :], st[:, SINKEXP, :]).then_inc(rinv_ready, 1)

                    def pT_rest(u):
                        dve.wait_ge(probs_turned, unit_no(hf, it, u) + 3)
                        for b in range(UNIT_BLK):
                            turned = turn_bank[u % 2][:, 2 * b * BLOCK:2 * (b + 1) * BLOCK]
                            for kb in range(2):
                                ins = nc.vector.tensor_tensor(
                                    parted[:, u % 2, b, kb], turned.rearrange("p (h q) -> p h q", h=2),
                                    in_block[:, kb].unsqueeze(1).to_broadcast([P, 2, BLOCK]), ALU.mult)
                            ins.then_inc(masked, 1)
                        for b in range(UNIT_BLK):
                            dve.wait_ge(pT_hi_ready, 2 * unit_no(hf, it, u) + b + 1)
                            nc.vector.tensor_tensor(pT_lo[:, b, :],
                                                    parted[:, u % 2, b].rearrange("p k h q -> p (k h q)"),
                                                    pT_hi[:, b, :].bitcast(F32), ALU.subtract).then_inc(pT_ready, 1)

                    def attn_out(u):
                        dve.wait_ge(shifted, unit_no(hf, it, u) + 1)
                        dve.wait_ge(squares_step, squares_count(hf, it))
                        ch, o = u // 2, (u % 2) * UNIT_BLK * BLOCK
                        cols = slice(o, o + UNIT_BLK * BLOCK)
                        for h in range(2):
                            rows = slice(HD * h, HD * h + HD)
                            ins = nc.vector.tensor_tensor(
                                attn_y[rows, ch, cols].rearrange("p (b q) -> p b q", q=BLOCK),
                                out_bank[rows, :, h, :], o_shift[rows], ALU.add)
                        ins.then_inc(attn_ready, 1)

                    def convolve(ch):
                        dve.wait_ge(evacuated[job_slot(hf, it, C, ch)], evac_count(hf, it, C, ch))
                        dve.wait_ge(job_done, job_no(hf, it, U, ch) + 1)
                        slot = job_slot(hf, it, U, ch)
                        o = ch * CHUNK
                        nc.vector.tensor_tensor(cu[:, 2 + o:2 + o + CHUNK], job_bank[slot][:], c_sb[:, ch, :],
                                                ALU.mult).then_inc(evacuated[slot], 1)
                        dve.wait_ge(evacuated[slot], evac_count(hf, it, U, ch))
                        step(nc.vector.tensor_scalar(taps[:], cu[:, o:o + CHUNK], conv_sb[:, it, 0:1], None,
                                                     ALU.mult))
                        for d in (1, 2):
                            step(nc.vector.scalar_tensor_tensor(out=taps[:], in0=cu[:, o + d:o + d + CHUNK],
                                                                scalar=conv_sb[:, it, d:d + 1], in1=taps[:],
                                                                op0=ALU.mult, op1=ALU.add))

                    def times_b(ch):
                        slot = job_slot(hf, it, B, ch)
                        dve.wait_ge(job_done, job_no(hf, it, B, ch) + 1)
                        dve.wait_ge(squares_step, squares_count(hf, it))
                        nc.vector.tensor_tensor(conv_y[:, ch, :], job_bank[slot][:], taps[:], ALU.mult
                                                ).then_inc(evacuated[slot], 1)
                        dve.wait_ge(evacuated[slot], evac_count(hf, it, B, ch))

                    def gate(j, ch):
                        slot = job_slot(hf, it, j, ch)
                        dve.wait_ge(tanh_ready, 2 * CHUNKS * (hf * TILES + it) + 2 * ch + (j - GC) + 1)
                        nc.vector.scalar_tensor_tensor(out=tanh_sb[:, ch, :], in0=tanh_sb[:, ch, :], scalar=1.0,
                                                       in1=job_bank[slot][:], op0=ALU.add, op1=ALU.mult
                                                       ).then_inc(evacuated[slot], 1)
                        dve.wait_ge(evacuated[slot], evac_count(hf, it, j, ch))

                    def apply_gate(y, branch, ch):
                        dve.wait_ge(stored[ch], 16 * (2 * (hf * TILES + it) + branch + 1))
                        nc.vector.scalar_tensor_tensor(out=gated[:, ch, :], in0=y[:, ch, :],
                                                       scalar=gains[:, branch, bass.ds(it, 1)],
                                                       in1=tanh_sb[:, ch, :], op0=ALU.mult, op1=ALU.mult
                                                       ).then_inc(gated_ready, 1)

                    ahead = last and hf == 0

                    nc.vector.tensor_scalar(sink_now[:], sink_bc[:, bass.ds(2 * it, 2)].unsqueeze(2).to_broadcast(
                        [P, 2, UNIT_BLK]), 1.0, None, ALU.mult)
                    step(nc.vector.tensor_scalar(cu[:, 0:2], cu_halo[:, it, :], 1.0, None, ALU.mult))
                    q_lo(0)
                    split_next(0)
                    q_lo(1)
                    split_next(1)
                    maxima(0)
                    denominators(0)
                    split_next(2)
                    maxima(1)
                    denominators(1)
                    convolve(0)
                    pT_rest(0)
                    split_next(3)
                    maxima(2)
                    if ahead:
                        variance(0, 2 * XT, XT)
                    denominators(2)
                    if ahead:
                        base_steps = steps[0]
                        steps[0] = base + k[0]
                        x_root(0, len(STAT_GROUPS) + 1, XT)
                        k[0] += NEWTON
                        steps[0] = base_steps
                    times_b(0)
                    convolve(1)
                    step(nc.vector.tensor_scalar(cu_halo[:, it, :], cu[:, HALF:HALF + 2], 1.0, None, ALU.mult))
                    attn_out(0)
                    pT_rest(1)
                    if ahead:
                        scale_x(1, 0)
                    gate(GC, 0)
                    apply_gate(conv_y, 0, 0)
                    if ahead:
                        gate(GA, 0)
                    maxima(3)
                    if ahead:
                        h_lo(1, 0)
                        scale_x(1, 1)
                    denominators(3)
                    if not ahead:
                        gate(GA, 0)
                    attn_out(1)
                    dve.wait_ge(attn_ready, unit_no(hf, it, 1) + 2)
                    apply_gate(attn_y, 1, 0)
                    pT_rest(2)
                    times_b(1)
                    split_next(4)
                    if ahead:
                        h_lo(1, 1)
                        scale_x(1, 2)
                        scale_x(1, 3)
                    gate(GC, 1)
                    apply_gate(conv_y, 0, 1)
                    split_next(5)
                    if ahead:
                        h_lo(1, 2)
                    attn_out(2)
                    pT_rest(3)
                    if ahead:
                        h_lo(1, 3)
                        scale_x(1, 4)
                    if last and hf == HALVES - 1:
                        mix_rest(0, 0)
                    gate(GA, 1)
                    if ahead:
                        scale_x(1, 5)
                    if last and hf == HALVES - 1:
                        wo_rest(0)
                    attn_out(3)
                    dve.wait_ge(attn_ready, unit_no(hf, it, 3) + 2)
                    apply_gate(attn_y, 1, 1)
                    step(nc.vector.tensor_scalar(bias[:], bias[:], 0.5, None, ALU.mult))
                    assert k[0] == VECTOR_STEPS + (NEWTON if ahead else 0)
                    if last:
                        steps[0] += k[0]
                    else:
                        steps[0] += VECTOR_STEPS * (PER_KV - g)

                tiles_of_half(dve, tile)

            for kt in range(1, MIX_KT):
                if kt == GROUP_KT:
                    mix_rest(1, 1)
                if kt == WO_EARLY:
                    dve.wait_ge(mix_summed, HALVES)
                    nc.vector.tensor_copy(mix_ssq[:, :, XT:TT],
                                          flat_out[:, 0:2 * XT].rearrange("p (s t) -> p s t", s=2)
                                          ).then_inc(mix_read, 1)
                wo_rest(kt)
            base_b = steps[0]

            def finish(p, t):
                first, final = isinstance(t, int) and t == 0, isinstance(t, int) and t == TT - 1
                k = [NEWTON if not first else 0]

                def step(ins):
                    k[0] += 1
                    ins.then_inc(dve_step, 1)
                    dve.wait_ge(dve_step, base_b + k[0] + (NEWTON + 2) * t)

                if not final and not (isinstance(t, int) and t < 2):
                    mix_rest(1 - p, t + 1)
                if first:
                    dve.wait_ge(mix_read, HALVES)
                    nc.vector.tensor_scalar(mix_ssq[:], mix_ssq[:], 1.0 / D_MODEL, EPS, ALU.mult, ALU.add
                                            ).then_inc(mix_var, 1)
                    dve.wait_ge(mix_rooted, 1)
                    newton(step, mix_r[:], mix_root[:], mix_ssq[:])
                dve.wait_ge(tile_done, t + 1)
                dve.wait_ge(res_landed[p], 8 * (t - p) + 16)
                for s in range(2):
                    for h in range(NH):
                        cols = slice(h * CHUNK, (h + 1) * CHUNK)
                        ins = nc.vector.scalar_tensor_tensor(
                            out=z[:, p, cols], in0=mix_bank[p][s][h], scalar=mix_r[:, s, bass.ds(t, 1)],
                            in1=z[:, p, cols], op0=ALU.mult, op1=ALU.add)
                    if s == 0:
                        step(ins)
                ins.then_inc(z_ready, 1)
                if first:
                    mix_rest(0, 2)
                dve.wait_ge(z_squared, t + 1)
                nc.vector.tensor_scalar(z_stat[:, p, 1:2], z_stat[:, p, 0:1], 1.0 / D_MODEL, EPS,
                                        ALU.mult, ALU.add).then_inc(z_var, 1)
                dve.wait_ge(z_rooted, t + 1)
                newton(step, z_stat[:, p, 3:4], z_stat[:, p, 2:3], z_stat[:, p, 1:2])
                if first:
                    dve.wait_ge(gain_landed, 32)
                nc.vector.scalar_tensor_tensor(out=z[:, p, :], in0=z[:, p, :], scalar=z_stat[:, p, 3:4],
                                               in1=gain_final[:], op0=ALU.mult, op1=ALU.mult
                                               ).then_inc(y_ready, 1)
                step(nc.vector.tensor_copy(z_stat[:, p, 0:1], z_stat[:, p, 3:4]))
                assert k[0] == 2 * NEWTON + 2

            tiles_of_tokens(dve, finish)

        @block.tensor
        def _(pe):
            pe.sem_inc(probs_turned, 2)
            pe.sem_inc(pv_done, 1)
            pe.wait_ge(pool_set, 2)

            def job(slot, bank, ch):
                cols = slice(ch * CHUNK, (ch + 1) * CHUNK)
                for kt in range(KT):
                    for n, (w, h) in enumerate(((w_hi, hT_hi), (w_hi, hT_lo), (w_lo, hT_hi))):
                        ins = nc.tensor.matmul(job_bank[bank][:], w[:, slot, kt, :], h[:, kt, cols],
                                               start=(kt == 0 and n == 0), stop=(kt == KT - 1 and n == 2))
                ins.then_inc(job_done, 1)

            def turn_x(hf, t):
                n = hf * XT + t
                tokens = x_first[t] if hf == 0 else x_sb[:, t % 2, :]
                pe.wait_ge(x_scaled, n + 1)
                for c in range(2):
                    if hf == 1 and t < len(X_AFTER):
                        use = BANK_USE["x", t, c]
                        pe.wait_ge(evacuated[use % RING], use // RING)
                    elif hf == 1 and t == len(X_AFTER):
                        pe.wait_ge(scores_read, unit_no(hf, 0, 0) + 1)
                    elif hf == 1 and t == len(X_AFTER) + 1:
                        pe.wait_ge(pT_ready, 2 * unit_no(hf, 0, 0) + 2)
                    elif t >= 2:
                        pe.wait_ge(h_ready, h_count(hf, t - 2))
                    for k in range(4):
                        kt = 4 * c + k
                        ins = nc.tensor.transpose(x_turn_bank(hf, t, c)[:, k * P:(k + 1) * P],
                                                  tokens[:, kt * P:(kt + 1) * P], ident[:])
                    ins.then_inc(x_turned, 1)

            def kv_job(hf, tile, ch):
                n, use = hf * HALF_TILES + tile, BANK_USE["kv", hf, tile, ch]
                pe.wait_ge(w_ready, n + 1)
                pe.wait_ge(h_ready, h_count(hf, (ch + 1) * CHUNK // P - 1))
                if use >= RING:
                    pe.wait_ge(evacuated[use % RING], use // RING)
                job(n % RING, use % RING, ch)

            def sum_squares(half):
                pe.wait_ge(squares_step, squares_count(half, TILES))
                pe.wait_ge(attn_ready, unit_no(half + 1, 0, 0) + 1)
                for s, ssq in enumerate((ssq_conv, ssq_attn)):
                    for t in range(XT):
                        o = t % (CHUNK // P) * P
                        ins = nc.tensor.matmul(flat_out[:, s * XT + t:s * XT + t + 1],
                                               ssq[:, t // (CHUNK // P), o:o + P], ones[:], start=True, stop=True)
                ins.then_inc(mix_summed, 1)

            for hf in range(HALVES):
                if hf == 0:
                    for t in range(4):
                        turn_x(0, t)
                else:
                    turn_x(1, 4)
                for i, (kv, ch) in enumerate(KV_ORDER):
                    if hf > 0 and i == 2:
                        sum_squares(hf - 1)
                    kv_job(hf, kv, ch)
                    for t in X_IN_KV[hf][i]:
                        turn_x(hf, t)
                for ch in range(CHUNKS):
                    use = BANK_USE["kv", hf, 1, ch]
                    pe.wait_ge(evacuated[use % RING], use // RING + 1)
                    pe.wait_ge(pT_ready, 2 * unit_no(hf, 0, 0) + 2)
                    for b in range(CHUNK // BLOCK):
                        ins = nc.tensor.transpose(turn_bank[ch][:, b * P:(b + 1) * P],
                                                  vT[:, ch, b * BLOCK:(b + 1) * BLOCK], ident[:])
                    ins.then_inc(v_turned, 1)

                def tile(it, g, i4):
                    last = isinstance(it, int)

                    def project(j, ch):
                        if ch == 0:
                            pe.wait_ge(w_ready, tile_no(hf, it, j) + 1)
                        slot = job_slot(hf, it, j, ch)
                        pe.wait_ge(evacuated[slot], evac_count(hf, it, j, ch) - 1)
                        job(tile_slot(hf, j), slot, ch)

                    def scores(u):
                        pe.wait_ge(k_ready, CHUNKS * (hf + 1) + hf)
                        pe.wait_ge(v_ready, CHUNKS * (hf + 1))
                        pe.wait_ge(evacuated[job_slot(hf, it, Q, u // 2)], evac_count(hf, it, Q, u // 2))
                        pe.wait_ge(scores_read, unit_no(hf, it, u) + 1)
                        for h in range(2):
                            for b in range(UNIT_BLK):
                                blk = UNIT_BLK * u + b
                                for part in range(2):
                                    ins = nc.tensor.matmul(
                                        score_bank[h][:, b, :], qs[:, h, blk * BLOCK:(blk + 1) * BLOCK],
                                        keys[:, g, part, blk * BLOCK:(blk + 2) * BLOCK],
                                        start=(part == 0), stop=(part == 1))
                        ins.then_inc(scores_done, 1)

                    def turn(u):
                        pe.wait_ge(probs_ready, unit_no(hf, it, u) + 1)
                        pe.wait_ge(pT_ready, 2 * unit_no(hf, it, u) + 2)
                        for b in range(UNIT_BLK):
                            for h in range(2):
                                o = (2 * b + h) * BLOCK
                                ins = nc.tensor.transpose(turn_bank[u % 2][:, o:o + BLOCK],
                                                          probs[:, u % 2, h, b, 0:BLOCK], ident[:])
                        ins.then_inc(probs_turned, 1)

                    def weigh(u):
                        pe.wait_ge(pT_ready, 2 * unit_no(hf, it, u) + 4)
                        pe.wait_ge(attn_ready, unit_no(hf, it, u) + 1)
                        if u == 0 and hf > 0:
                            pe.wait_ge(mix_read, hf)
                        for b in range(UNIT_BLK):
                            n = 0
                            for kb in range(2):
                                for pT in (pT_hi, pT_lo):
                                    ins = nc.tensor.matmul(
                                        out_bank[:, b, :, :].rearrange("p h q -> p (h q)"),
                                        vals[:, UNIT_BLK * u + b + kb, g, :, :].rearrange("p s d -> p (s d)"),
                                        pT[:, b, 2 * kb * BLOCK:2 * (kb + 1) * BLOCK],
                                        start=(n == 0), stop=(n == 3))
                                    n += 1
                        ins.then_inc(pv_done, 1)

                    ahead = last and hf == 0

                    project(Q, 0)
                    project(Q, 1)
                    scores(0)
                    project(C, 0)
                    project(C, 1)
                    scores(1)
                    project(U, 0)
                    turn(0)
                    project(U, 1)
                    scores(2)
                    project(B, 0)
                    weigh(0)
                    turn(1)
                    project(GC, 0)
                    scores(3)
                    project(GA, 0)
                    if ahead:
                        turn_x(1, 0)
                    weigh(1)
                    turn(2)
                    project(B, 1)
                    if ahead:
                        turn_x(1, 1)
                    project(GC, 1)
                    if ahead:
                        turn_x(1, 2)
                    weigh(2)
                    turn(3)
                    if ahead:
                        turn_x(1, 3)
                    project(GA, 1)
                    weigh(3)

                tiles_of_half(pe, tile)

            def products(p, kt):
                s = kt // TILES
                for n, (m, part) in enumerate(((mix_hi, 0), (mix_hi, 1), (mix_lo, 0))):
                    for h in range(NH):
                        ins = nc.tensor.matmul(mix_bank[p][s][h], m[:, p, kt, :],
                                               wo_part(kt, part)[:, h * CHUNK:(h + 1) * CHUNK],
                                               start=(kt % TILES == 0 and n == 0),
                                               stop=(kt % TILES == TILES - 1 and n == 2))
                return ins

            def first_pair():
                for slot in range(RING):
                    uses = BANK_USE["last", HALVES - 1, ITER_JOBS - 1] + 1
                    pe.wait_ge(evacuated[slot], (uses - 1 - slot) // RING + 1)
                pe.wait_ge(scores_read, unit_no(HALVES, 0, 0) + 1)
                for g in range(MIX_KT // GROUP_KT + 1):
                    for p in (1, 0):
                        if not 0 <= g - p < MIX_KT // GROUP_KT:
                            continue
                        if g == p:
                            pe.wait_ge(mix_ready, p + 1)
                        if (p, g) == (1, 1):
                            pe.wait_ge(pT_ready, 2 * unit_no(HALVES, 0, 0) + 2)
                        for kt in range(GROUP_KT * (g - p), GROUP_KT * (g - p + 1)):
                            if p == 0:
                                pe.wait_ge(wo_ready, kt + 1)
                            if (p, kt) == (1, WO_EARLY):
                                pe.wait_ge(mix_read, HALVES)
                            ins = products(p, kt)
                            if (p, kt) == (0, GROUP_KT - 1):
                                sum_squares(HALVES - 1)
                        if g - p == MIX_KT // GROUP_KT - 1:
                            ins.then_inc(tile_done, 1)

            def multiply(p, t):
                if isinstance(t, int) and t < 2:
                    if t == 0:
                        first_pair()
                    return
                pe.wait_ge(mix_ready, t + 1)
                pe.wait_ge(z_ready, t - 1)
                for kt in range(MIX_KT):
                    ins = products(p, kt)
                ins.then_inc(tile_done, 1)

            tiles_of_tokens(pe, multiply)


def kernel(x, norm_in, w_in, conv_w, attn_sinks, norm_conv_out, norm_attn_out, w_out, norm_final):
    import numpy as np
    import concourse.bacc as bacc
    from concourse.bass_utils import run_bass_kernel_spmd

    kv = 5 * TILES
    order = [kv, kv + 1]
    for i in range(TILES):
        order += [4 * TILES + i, TILES + i, 2 * TILES + i, i, 3 * TILES + i, kv + 2 + i]
    w_tiles = np.asarray(w_in)[0].reshape(KT, P, HALF_TILES, P).transpose(2, 1, 0, 3)[order]
    arrays = {
        "x": np.asarray(x)[0],
        "norm_in": np.asarray(norm_in),
        "w_in": w_tiles.reshape(len(order), P, KT * P),
        "conv_w": np.asarray(conv_w)[0].reshape(3, TILES, P).transpose(2, 1, 0),
        "sinks": np.asarray(attn_sinks),
        "gain_conv": np.asarray(norm_conv_out)[0].reshape(TILES, P).T,
        "gain_attn": np.asarray(norm_attn_out)[0].reshape(TILES, P).T,
        "w_out": np.asarray(w_out)[0].reshape(MIX_KT, P, D_MODEL),
        "norm_final": np.asarray(norm_final)[None],
    }
    arrays = {n: np.ascontiguousarray(a) for n, a in arrays.items()}
    nc = bacc.Bacc("TRN2", target_bir_lowering=False, num_devices=1)
    args = [nc.dram_tensor(n, list(a.shape), F32, kind="ExternalInput").ap() for n, a in arrays.items()]
    out = nc.dram_tensor("out", [SEQ, D_MODEL], F32, kind="ExternalOutput").ap()
    build(nc, *args, out)
    r = run_bass_kernel_spmd(nc, [arrays], core_ids=[0])
    return r.results[0]["out"].reshape(1, SEQ, D_MODEL)
```
